# Optimizing a Trainium2 kernel written in Bass

```python
import jax, jax.numpy as jnp
from jax import lax
import numpy as np

D_MODEL = 1024
BATCH = 1
SEQ = 1024
DEPTH = 1
DEC_BATCH = 1
DEC_SEQ = 64
PAST_LEN = 2048

CHUNK = 64
SB_HEADS = 16
SB_HEAD_DIM = 64
SB_WIDTH = SB_HEADS * SB_HEAD_DIM
SB_BLOCK = 128
GM_GROUPS = 8
GM_GROUP_DIM = 128
GM_WIDTH = GM_GROUPS * GM_GROUP_DIM
GM_CHUNK = 128
D_FF = 2816
CONV_WIDTH = 3
EPS = 1e-6
IN_WIDTH = 2 * GM_WIDTH + 3 * SB_WIDTH

kernel_name = "hybrid_stream_gmlp_stickbreak_convffn"

def rms_norm(x, g):
    xf = x.astype(jnp.float32)
    xf = xf * lax.rsqrt(jnp.mean(xf * xf, axis=-1, keepdims=True) + EPS)
    return xf.astype(x.dtype) * g

def layer_norm(x, g, b):
    xf = x.astype(jnp.float32)
    mu = jnp.mean(xf, axis=-1, keepdims=True)
    var = jnp.mean(jnp.square(xf - mu), axis=-1, keepdims=True)
    return ((xf - mu) * lax.rsqrt(var + EPS)).astype(x.dtype) * g + b

def spatial_gating(u, v, w_s, b_s):
    bsz, t, _ = v.shape
    n_pos = min(t, GM_CHUNK)
    n_chunks = t // n_pos
    tri = jnp.tril(jnp.ones((n_pos, n_pos), dtype=bool))
    w = jnp.where(tri[None], w_s[:, :n_pos, :n_pos], 0.0)
    vc = v.reshape(bsz, n_chunks, n_pos, GM_GROUPS, GM_GROUP_DIM)
    mixed = jnp.einsum('gts,bcsgd->bctgd', w, vc) + b_s[:, :n_pos].T[None, None, :, :, None]
    return u * mixed.reshape(bsz, t, GM_WIDTH)

def stick_breaking(q, k, v, q_offset):
    tq = q.shape[1]
    scale = SB_HEAD_DIM ** -0.5
    outs = []
    for start in range(0, tq, SB_BLOCK):
        stop = min(start + SB_BLOCK, tq)
        n_keys = q_offset + stop
        qb = q[:, start:stop].astype(jnp.float32)
        kb = k[:, :n_keys].astype(jnp.float32)
        vb = v[:, :n_keys]
        z = jnp.einsum('bqhd,bkhd->bhqk', qb, kb) * scale
        qpos = q_offset + start + jnp.arange(stop - start)
        kpos = jnp.arange(n_keys)
        mask = kpos[None, :] < qpos[:, None]
        log_one_minus = jnp.where(mask, jax.nn.log_sigmoid(-z), 0.0)
        after = lax.cumsum(log_one_minus, axis=3, reverse=True) - log_one_minus
        a = jnp.where(mask, jnp.exp(jax.nn.log_sigmoid(z) + after), 0.0)
        outs.append(jnp.einsum('bhqk,bkhd->bqhd', a.astype(v.dtype), vb))
    return jnp.concatenate(outs, axis=1)

def layer(x, past_k, past_v, conv_prev, q_offset,
          g_pre_mix, w_in, ln_v_g, ln_v_b, w_s, b_s, w_gate, b_gate, w_branch_a, w_branch_b, w_o,
          g_post_mix, g_pre_ffn, w_up, w_conv, b_conv, w_down, g_post_ffn):
    bsz, t, _ = x.shape
    h = rms_norm(x, g_pre_mix)
    proj = h @ w_in
    u_a, v_a, q, k, v_b = jnp.split(
        proj, [GM_WIDTH, 2 * GM_WIDTH, 2 * GM_WIDTH + SB_WIDTH, 2 * GM_WIDTH + 2 * SB_WIDTH], axis=-1)
    u_a = jax.nn.gelu(u_a)
    v_a = layer_norm(jax.nn.gelu(v_a), ln_v_g, ln_v_b)
    y_a = spatial_gating(u_a, v_a, w_s, b_s)
    q = q.reshape(bsz, t, SB_HEADS, SB_HEAD_DIM)
    k = k.reshape(bsz, t, SB_HEADS, SB_HEAD_DIM)
    v_b = v_b.reshape(bsz, t, SB_HEADS, SB_HEAD_DIM)
    if past_k is None:
        k_all, v_all = k, v_b
    else:
        k_all = jnp.concatenate([past_k, k], axis=1)
        v_all = jnp.concatenate([past_v, v_b], axis=1)
    y_b = stick_breaking(q, k_all, v_all, q_offset).reshape(bsz, t, SB_WIDTH)
    gates = jax.nn.sigmoid(h @ w_gate + b_gate)
    g_a, g_b = jnp.split(gates, 2, axis=-1)
    merged = g_a * (y_a @ w_branch_a) + g_b * (y_b @ w_branch_b)
    x = x + rms_norm(merged @ w_o, g_post_mix)
    up = rms_norm(x, g_pre_ffn) @ w_up
    buf = jnp.concatenate([conv_prev.astype(up.dtype), up], axis=1)
    conv = b_conv + sum(w_conv[i] * buf[:, i:i + t] for i in range(CONV_WIDTH))
    gate, val = jnp.split(conv, 2, axis=-1)
    ff = (jax.nn.gelu(gate) * val) @ w_down
    x = x + rms_norm(ff, g_post_ffn)
    return x, k, v_b, buf[:, -(CONV_WIDTH - 1):], v_a

def setup_inputs(seed: int = 0) -> dict:
    key = jax.random.key(seed)
    ks = jax.random.split(key, 32)
    f32 = jnp.float32

    def nrm(k, shape, scale):
        return jax.random.normal(k, shape, f32) * scale

    def gain(k, shape):
        return 1.0 + 0.02 * jax.random.normal(k, shape, f32)

    L = DEPTH
    return {
        "x_prompt": nrm(ks[0], (BATCH, SEQ, D_MODEL), 1.0),
        "x_sample": nrm(ks[1], (DEC_BATCH, DEC_SEQ, D_MODEL), 1.0),
        "cache_sb_k": nrm(ks[2], (L, DEC_BATCH, PAST_LEN, SB_HEADS, SB_HEAD_DIM), 1.0),
        "cache_sb_v": nrm(ks[3], (L, DEC_BATCH, PAST_LEN, SB_HEADS, SB_HEAD_DIM), 1.0),
        "state_ffn_conv": nrm(ks[4], (L, DEC_BATCH, CONV_WIDTH - 1, 2 * D_FF), 1.0),
        "g_pre_mix": gain(ks[5], (L, D_MODEL)),
        "w_in": nrm(ks[6], (L, D_MODEL, IN_WIDTH), D_MODEL ** -0.5),
        "ln_v_g": gain(ks[7], (L, GM_WIDTH)),
        "ln_v_b": nrm(ks[8], (L, GM_WIDTH), 0.02),
        "w_s": nrm(ks[9], (L, GM_GROUPS, GM_CHUNK, GM_CHUNK), 0.5 * GM_CHUNK ** -0.5),
        "b_s": gain(ks[10], (L, GM_GROUPS, GM_CHUNK)),
        "w_gate": nrm(ks[11], (L, D_MODEL, 2 * D_MODEL), D_MODEL ** -0.5),
        "b_gate": nrm(ks[12], (L, 2 * D_MODEL), 0.01),
        "w_branch_a": nrm(ks[13], (L, GM_WIDTH, D_MODEL), GM_WIDTH ** -0.5),
        "w_branch_b": nrm(ks[14], (L, SB_WIDTH, D_MODEL), SB_WIDTH ** -0.5),
        "w_o": nrm(ks[15], (L, D_MODEL, D_MODEL), D_MODEL ** -0.5),
        "g_post_mix": gain(ks[16], (L, D_MODEL)),
        "g_pre_ffn": gain(ks[17], (L, D_MODEL)),
        "w_up": nrm(ks[18], (L, D_MODEL, 2 * D_FF), D_MODEL ** -0.5),
        "w_conv": nrm(ks[19], (L, CONV_WIDTH, 2 * D_FF), CONV_WIDTH ** -0.5),
        "b_conv": nrm(ks[20], (L, 2 * D_FF), 0.02),
        "w_down": nrm(ks[21], (L, D_FF, D_MODEL), D_FF ** -0.5),
        "g_post_ffn": gain(ks[22], (L, D_MODEL)),
    }

def reference(x_prompt, x_sample, cache_sb_k, cache_sb_v, state_ffn_conv,
              g_pre_mix, w_in, ln_v_g, ln_v_b, w_s, b_s, w_gate, b_gate, w_branch_a, w_branch_b, w_o,
              g_post_mix, g_pre_ffn, w_up, w_conv, b_conv, w_down, g_post_ffn):
    y_p, y_s = x_prompt, x_sample
    k_p, v_p, c_p, k_s, v_s, c_s, gv_s = [], [], [], [], [], [], []
    for l in range(DEPTH):
        params = (g_pre_mix[l], w_in[l], ln_v_g[l], ln_v_b[l], w_s[l], b_s[l], w_gate[l], b_gate[l],
                  w_branch_a[l], w_branch_b[l], w_o[l], g_post_mix[l], g_pre_ffn[l], w_up[l],
                  w_conv[l], b_conv[l], w_down[l], g_post_ffn[l])
        zero_conv = jnp.zeros((y_p.shape[0], CONV_WIDTH - 1, 2 * D_FF), y_p.dtype)
        y_p, kp, vp, cp, _ = layer(y_p, None, None, zero_conv, 0, *params)
        past_len = cache_sb_k.shape[2]
        y_s, ks_, vs_, cs_, gvs = layer(y_s, cache_sb_k[l], cache_sb_v[l], state_ffn_conv[l], past_len, *params)
        k_p.append(kp); v_p.append(vp); c_p.append(cp)
        k_s.append(ks_); v_s.append(vs_); c_s.append(cs_); gv_s.append(gvs)
    new_sb_k_prompt = jnp.stack(k_p)
    new_sb_v_prompt = jnp.stack(v_p)
    new_conv_prompt = jnp.stack(c_p)
    new_sb_k_sample = jnp.stack(k_s)
    new_sb_v_sample = jnp.stack(v_s)
    new_conv_sample = jnp.stack(c_s)
    new_gmlp_v_sample = jnp.stack(gv_s)
    return (y_p, y_s, new_sb_k_prompt, new_sb_v_prompt, new_conv_prompt,
            new_sb_k_sample, new_sb_v_sample, new_conv_sample, new_gmlp_v_sample)


_drawn_inputs = setup_inputs


def setup_inputs(seed=0):
    import zlib

    import numpy as np

    out = dict(_drawn_inputs(seed))
    spreads = {}
    factors = {'ln_v_g': 22.955,
     'ln_v_b': 24.162,
     'b_s': 5.163,
     'b_gate': 8.0,
     'g_post_mix': 3.481,
     'g_pre_ffn': 2.776,
     'b_conv': 3.462,
     'g_post_ffn': 49.63,
     'cache_sb_k': 3.872}
    for name, (base, spread) in spreads.items():
        noise = np.random.default_rng([zlib.crc32(name.encode()), seed]).standard_normal(out[name].shape)
        drawn = base * np.exp(spread * noise) if base else spread * noise
        out[name] = __import__('jax').numpy.asarray(drawn.astype(out[name].dtype))
    for name, factor in factors.items():
        out[name] = (out[name] * factor).astype(out[name].dtype)
    return out
```

```python
from contextlib import ExitStack

import concourse.bass as bass
from concourse import mybir
from concourse.alu_op_type import AluOpType as ALU

ACT = mybir.ActivationFunctionType
F32 = mybir.dt.float32
F32R = mybir.dt.float32r
I32 = mybir.dt.int32

P = 128
D = 1024
KT = D // P
SEQ, DEC, PAST = 1024, 64, 2048
HEADS, DH = 16, 64
PAIRS = HEADS // 2
GROUPS = 8
FF = 2816
FT = FF // P
GAP = 2
COLS = GAP + SEQ + GAP + DEC
NCH = 3
CH = COLS // NCH
SCOL = GAP + SEQ + GAP
TILES = SEQ // P + 1
SLOT = 1024
EPS = 1e-6
SCALE = DH ** -0.5
RSQRT_MAGIC = float(0x5F3759DF)


def rows(m):
    return P if m < TILES - 1 else DEC


def col(m):
    return GAP + m * P if m < TILES - 1 else SCOL


class Place:

    def __init__(self, nc, start, size):
        self.nc, self.at, self.end = nc, start, start + size

    def __call__(self, name, shape, dtype=F32):
        size = 4
        for n in shape[1:]:
            size *= n
        t = self.nc.alloc_sbuf_tensor_at(name, shape, dtype, offset=self.at)
        self.at += (size + 31) // 32 * 32
        assert self.at <= self.end, (name, self.at - self.end)
        return t


class Sems:

    def __init__(self, nc, stack, phase):
        self.nc, self.phase, self.known = nc, phase, {}
        stack.callback(self.give_back)

    def give_back(self):
        self.nc.clear_and_free_semaphores(list(self.known.values()))
        self.nc.all_engine_barrier()

    def __call__(self, name):
        if name not in self.known:
            self.known[name] = self.nc.alloc_semaphore(f"{self.phase}_{name}")
        return self.known[name]


class Chain:

    def __init__(self, eng, sem, start=0):
        self.eng, self.sem, self.n = eng, sem, start

    def step(self, ins):
        self.n += 1
        ins.then_inc(self.sem, 1)
        self.eng.wait_ge(self.sem, self.n)


class Weights:

    CREDIT = 4

    def __init__(self, nc, s, phase, slots, raw_place, place):
        self.nc, self.slots = nc, slots
        self.raw = raw_place(f"{phase}_w_raw", [P, 2, SLOT])
        self.hi = place(f"{phase}_w_hi", [P, slots, SLOT], F32R)
        self.lo = place(f"{phase}_w_lo", [P, slots, SLOT], F32R)
        self.raw_ready = [s("raw_ready0"), s("raw_ready1")]
        self.split, self.passed = s("weights_split"), s("split_passed")

    def start_pool(self, pool):
        pool.sem_inc(self.split, self.CREDIT)

    def load(self, sp, n, parity, src, tiles):
        sp.wait_ge(self.split, n * 2 + 2)
        sp.dma_start(self.raw[:, parity, :].rearrange("p (k c) -> p k c", k=tiles), src).then_inc(self.raw_ready[parity], 16)

    def split_one(self, pool, n, uses, slot, parity):
        pool.wait_ge(self.raw_ready[parity], (uses + 1) * 16)
        hold(pool, self.passed)
        self.nc.gpsimd.tensor_scalar(self.hi[:, slot, :], self.raw[:, parity, :], 1.0, 0.0,
                                     ALU.mult, ALU.add).then_inc(self.split, 1)
        pool.wait_ge(self.split, n * 2 + (self.CREDIT + 1))
        self.nc.gpsimd.tensor_tensor(self.lo[:, slot, :], self.raw[:, parity, :],
                                     self.hi[:, slot, :].bitcast(F32), ALU.subtract).then_inc(self.split, 1)

    def ready(self, pe, n):
        pe.wait_ge(self.split, n * 2 + (self.CREDIT + 2))


def hold(eng, passed):
    eng.sem_inc(passed)


def three_passes(nc, out, stat_hi, stat_lo, mov_hi, mov_lo, first, last):
    nc.tensor.matmul(out, stat_hi, mov_lo, start=first, stop=False)
    nc.tensor.matmul(out, stat_hi, mov_hi, start=False, stop=False)
    return nc.tensor.matmul(out, stat_lo, mov_hi, start=False, stop=last)


def rsqrt_steps(nc, chain, v, y, t, scale):
    vec = nc.vector
    chain.step(vec.tensor_scalar(v, v, scale, EPS, ALU.mult, ALU.add))
    chain.step(vec.tensor_scalar(t.bitcast(I32), v.bitcast(I32), 1, None, ALU.logical_shift_right))
    chain.step(vec.tensor_scalar(y.bitcast(I32), t.bitcast(I32), -1.0, RSQRT_MAGIC, ALU.mult, ALU.add))
    for _ in range(3):
        chain.step(vec.scalar_tensor_tensor(out=t, in0=y, scalar=-0.5, in1=y, op0=ALU.mult, op1=ALU.mult))
        chain.step(vec.tensor_tensor(t, t, v, ALU.mult))
        chain.step(vec.scalar_tensor_tensor(out=y, in0=t, scalar=1.5, in1=y, op0=ALU.add, op1=ALU.mult))


def clear_gaps(nc, eng, *arrays):
    for a in arrays:
        eng.memset(a[:, :, 0:GAP].bitcast(F32), 0.0)
        last = eng.memset(a[:, :, GAP + SEQ:SCOL].bitcast(F32), 0.0)
    return last


PAR = {"b_gate": 0, "b_s": 16, "b_conv": 24, "w_conv0": 128, "w_conv1": 172, "w_conv2": 256,
       "state0": 384, "state1": 428}


def build_layer(nc, a, o):
    base = (nc.sbuf_base + 63) // 64 * 64
    small = Place(nc, base, 3072)
    region = COLS * KT * 4 * 2
    r0 = base + 3072
    r1 = r0 + region
    rf = r1 + region
    f_size = nc.sbuf_usable_end - rf
    ident = small("ident", [P, P])
    par = small("par", [P, 512])

    def dram(name, shape):
        return nc.dram_tensor(name, shape, F32, kind="Internal").ap()

    u_dram = dram("u_scratch", (SEQ + DEC, D))
    q_dram = dram("q_scratch", (SEQ + DEC, D))
    ta_dram = dram("ta_scratch", (KT, P, COLS))
    gb_dram = dram("gb_scratch", (KT, P, COLS))
    x2_dram = dram("x2_scratch", (SEQ + DEC, D))

    def pair_of(name, start):
        pl = Place(nc, start, region)
        return pl(name + "_hi", [P, KT, COLS], F32R), pl(name + "_lo", [P, KT, COLS], F32R)

    hT = pair_of("hT", r0)
    yaT = pair_of("yaT", r1)
    ybT = pair_of("ybT", r0)
    mgT = pair_of("mergedT", r1)
    v_tok = nc.alloc_sbuf_tensor_at("v_tok", [P, TILES, D], F32, offset=rf)
    v_bytes = TILES * D * 4

    phase_project(nc, a, o, ident, par, hT, v_tok, u_dram, q_dram, r1, region, rf + v_bytes, f_size - v_bytes)
    phase_gating(nc, a, o, ident, par, v_tok, yaT, u_dram, rf + v_bytes, f_size - v_bytes)
    phase_gates(nc, a, par, hT, yaT, ta_dram, gb_dram, rf, f_size)
    phase_prompt_attention(nc, o, ident, ybT, q_dram, r1, region + f_size)
    phase_sample_attention(nc, a, o, ident, ybT, q_dram, r1, region + f_size)
    phase_merge(nc, a, ybT, mgT, ta_dram, gb_dram, rf, f_size)
    phase_output(nc, a, ident, mgT, x2_dram, r0, region, rf, f_size)
    phase_ffn(nc, a, o, ident, par, mgT, x2_dram, r0, region, rf, f_size)


def phase_project(nc, a, o, ident, par, hT, v_tok, u_dram, q_dram, r1, r1_size, rf, rf_size):
    w_in = a["w_in"][0].rearrange("(k p) c -> p k c", p=P)
    with ExitStack() as ctx:
        s = Sems(nc, ctx, "p1")
        f = Place(nc, rf, rf_size)
        ring_place = Place(nc, r1, r1_size)
        ring = Weights(nc, s, "p1", 8, f, ring_place)
        par_rows = ring_place("par_rows", [P, 4, P])
        g_row = f("g_pre_row", [P, D])
        lng = f("ln_g_row", [P, D])
        lnb = f("ln_b_row", [P, D])
        stage = f("stage", [P, 3, 512])
        ss = f("ss", [P, TILES])
        rstd = f("rstd", [P, TILES])
        tmp = f("rs_tmp", [P, TILES])
        stats = f("stats", [P, 2, 6])
        mv = f("mean_var", [P, TILES, 2])
        psA = ctx.enter_context(nc.psum_tensor("p1_psA", [P, 2, KT, P], F32))
        psB = ctx.enter_context(nc.psum_tensor("p1_psB", [P, 3, 512], F32))
        psP = ctx.enter_context(nc.psum_tensor("p1_psP", [P, 512], F32))
        x_tok = nc.alloc_sbuf_tensor_at("x_tok", [P, TILES, D], F32, offset=rf - TILES * D * 4)
        NM = 5
        with nc.Block() as block:

            @block.sync
            def _(sp):
                for m in range(TILES):
                    src = a["x_prompt"][0, m * P:(m + 1) * P, :] if m < TILES - 1 else a["x_sample"][0]
                    sp.dma_start(x_tok[0:rows(m), m, :], src).then_inc(s(f"x_ready{m}"), 16)
                sp.dma_start(g_row[:, :], a["g_pre_mix"].to_broadcast([P, D])).then_inc(s("g_ready"), 16)
                with sp.Fori(0, NM) as i:
                    for n in range(8):
                        src = w_in[:, 2 * (n % 4):2 * (n % 4) + 2, bass.ds(i * D + (n // 4) * 512, 512)]
                        ring.load(sp, i * 8 + n, n % 2, src, 2)

            @block.gpsimd
            def _(pool):
                ring.start_pool(pool)
                nc.gpsimd.memset(ident[:], 0.0).then_inc(s("ident"), 1)
                pool.wait_ge(s("ident"), 1)
                nc.gpsimd.affine_select(out=ident[:], in_=ident[:], compare_op=ALU.not_equal, fill=1.0, base=0,
                                        pattern=[[-1, P]], channel_multiplier=1).then_inc(s("ident"), 1)
                with pool.Fori(0, NM) as i:
                    for n in range(8):
                        if n % 4 == 0:
                            pool.wait_ge(s("proj_ready"), i * 2 * TILES + (n // 4 + 1) * TILES)
                        ring.split_one(pool, i * 8 + n, i * 4 + n // 2, n, n % 2)

            @block.tensor
            def _(pe):
                pe.sem_inc(s("proj_ready"), 2 * TILES)
                pe.wait_ge(s("ident"), 2)
                pe.wait_ge(s("par_ready"), 16 * 8)
                for g in range(4):
                    last = nc.tensor.transpose(psP[:, g * P:(g + 1) * P], par_rows[:, g, :], ident[:, :])
                last.then_inc(s("par_turned"), 1)
                for m in range(TILES):
                    pe.wait_ge(s("h_ready"), m + 1)
                    if m >= 2:
                        pe.wait_ge(s("hT_hi"), m - 1)
                        pe.wait_ge(s("hT_lo"), m - 1)
                    for k in range(KT):
                        last = nc.tensor.transpose(psA[:, m % 2, k, 0:rows(m)], x_tok[0:rows(m), m, k * P:(k + 1) * P],
                                                   ident[0:rows(m), 0:rows(m)])
                    last.then_inc(s("h_turned"), 1)
                pe.wait_ge(s("hT_hi"), TILES)
                pe.wait_ge(s("hT_lo"), TILES)
                with pe.Fori(0, NM) as i:
                    for c in range(2):
                        ring.ready(pe, i * 8 + 4 * c + 3)
                        for m in range(TILES):
                            n = c * TILES + m
                            pe.wait_ge(s("proj_free"), i * 2 * TILES + n + 1)
                            for k in range(KT):
                                slot, at = 4 * c + k // 2, (k % 2) * 512
                                last = three_passes(
                                    nc, psB[0:rows(m), n % 3, :], hT[0][:, k, col(m):col(m) + rows(m)],
                                    hT[1][:, k, col(m):col(m) + rows(m)], ring.hi[:, slot, at:at + 512],
                                    ring.lo[:, slot, at:at + 512], k == 0, k == KT - 1)
                            last.then_inc(s("proj_ready"), 1)

            @block.scalar
            def _(act):
                act.sem_inc(s("proj_free"), 3)
                for b in range(3):
                    act.sem_inc(s(f"stage_free{b}"), 16)
                act.wait_ge(s("par_zero"), 1)
                for src, g, r, n in (("b_gate", 0, 0, 16), ("b_s", 0, 16, 8), ("b_conv", 0, 24, 44)):
                    v = a[src][0] if src == "b_s" else a[src][0].rearrange("(r c) -> r c", c=P)
                    act.dma_start(par_rows[r:r + n, g, :], v).then_inc(s("par_ready"), 16)
                for j, (g, r) in enumerate(((1, 0), (1, 44), (2, 0))):
                    act.dma_start(par_rows[r:r + 44, g, :], a["w_conv"][0, j].rearrange("(r c) -> r c", c=P)).then_inc(s("par_ready"), 16)
                for j in range(2):
                    act.dma_start(par_rows[44 * j:44 * j + 44, 3, :],
                                  a["state_ffn_conv"][0, 0, j].rearrange("(r c) -> r c", c=P)).then_inc(s("par_ready"), 16)
                act.dma_start(lng[:, :], a["ln_v_g"].to_broadcast([P, D])).then_inc(s("ln_ready"), 16)
                act.dma_start(lnb[:, :], a["ln_v_b"].to_broadcast([P, D])).then_inc(s("ln_ready"), 16)
                act.wait_ge(s("ss_zero"), 1)
                for m in range(TILES):
                    act.wait_ge(s(f"x_ready{m}"), 16)
                    nc.scalar.activation(psA[0:rows(m), 0].rearrange("p k c -> p (k c)"), x_tok[0:rows(m), m, :],
                                         ACT.Square, accum_out=ss[0:rows(m), m:m + 1]).then_inc(s("squares"), 1)
                    act.wait_ge(s("squares"), m + 1)
                for m in range(TILES):
                    act.wait_ge(s("h_turned"), m + 1)
                    nc.scalar.activation(hT[0][:, :, col(m):col(m) + rows(m)], psA[:, m % 2, :, 0:rows(m)],
                                         ACT.Copy).then_inc(s("hT_hi"), 1)

                def empty(first, func, where):
                    with act.Fori(0, 2) as c:
                        for m in range(TILES):
                            n = c * TILES + (first * 2 * TILES + m)
                            act.wait_ge(s("proj_ready"), n + (2 * TILES + 1))
                            if where is None:
                                nc.scalar.activation(v_tok[0:rows(m), m, bass.ds(c * 512, 512)], psB[0:rows(m), m % 3, :],
                                                     func).then_inc(s("proj_free"), 1)
                                continue
                            b = m % 3
                            use = (first - (first > 1)) * 6 + m // 3
                            act.wait_ge(s(f"stage_free{b}"), (c * 3 + (use + 1)) * 16)
                            nc.scalar.activation(stage[0:rows(m), b, :], psB[0:rows(m), m % 3, :],
                                                 func).then_inc(s("proj_free"), 1)
                            act.wait_ge(s("proj_free"), n + 4)
                            act.dma_start(where(m, c), stage[0:rows(m), b, :]).then_inc(s(f"stage_free{b}"), 16)

                def rows_of(dst):
                    return lambda m, c: dst[m * P:m * P + rows(m), bass.ds(c * 512, 512)]

                def out_rows(prompt, sample):
                    pr = prompt[0, 0].rearrange("t h d -> t (h d)")
                    sa = sample[0, 0].rearrange("t h d -> t (h d)")
                    return lambda m, c: (pr[m * P:(m + 1) * P, bass.ds(c * 512, 512)] if m < TILES - 1
                                         else sa[:, bass.ds(c * 512, 512)])

                empty(0, ACT.Gelu_apprx_tanh, rows_of(u_dram))
                empty(1, ACT.Gelu_apprx_tanh, None)
                empty(2, ACT.Copy, rows_of(q_dram))
                empty(3, ACT.Copy, out_rows(o["new_sb_k_prompt"], o["new_sb_k_sample"]))
                empty(4, ACT.Copy, out_rows(o["new_sb_v_prompt"], o["new_sb_v_sample"]))
                for b in range(3):
                    act.wait_ge(s(f"stage_free{b}"), 16 * (1 + 4 * 6))
                act.wait_ge(s("v_normed"), TILES)
                act.dma_start(o["new_gmlp_v_sample"][0, 0], v_tok[0:DEC, TILES - 1, :]).then_inc(s("gv_stored"), 16)
                act.wait_ge(s("gv_stored"), 16)

            @block.vector
            def _(dve):
                ch = Chain(dve, s("dve_chain"))
                nc.vector.memset(par_rows[:], 0.0).then_inc(s("par_zero"), 1)
                ch.step(nc.vector.memset(ss[:], 1.0))
                nc.vector.sem_inc(s("ss_zero"), 1)
                ch.step(clear_gaps(nc, nc.vector, *hT))
                dve.wait_ge(s("par_turned"), 1)
                nc.vector.tensor_copy(par[:], psP[:]).then_inc(s("par_copied"), 1)
                dve.wait_ge(s("squares"), TILES)
                rsqrt_steps(nc, ch, ss[:], rstd[:], tmp[:], 1.0 / D)
                dve.wait_ge(s("g_ready"), 16)
                for m in range(TILES):
                    r = rows(m)
                    nc.vector.scalar_tensor_tensor(out=x_tok[0:r, m, :], in0=x_tok[0:r, m, :], scalar=rstd[0:r, m:m + 1],
                                                   in1=g_row[0:r, :], op0=ALU.mult, op1=ALU.mult).then_inc(s("h_ready"), 1)
                for m in range(TILES):
                    c = slice(col(m), col(m) + rows(m))
                    dve.wait_ge(s("hT_hi"), m + 1)
                    nc.vector.tensor_tensor(hT[1][:, :, c], psA[:, m % 2, :, 0:rows(m)], hT[0][:, :, c].bitcast(F32),
                                            ALU.subtract).then_inc(s("hT_lo"), 1)
                dve.wait_ge(s("ln_ready"), 32)
                ch.step(nc.vector.memset(mv[:], 1.0))
                for m in range(TILES):
                    r = rows(m)
                    dve.wait_ge(s("proj_free"), 3 + 2 * TILES + TILES + m + 1)
                    for h in range(2):
                        ch.step(nc.vector.bn_stats(stats[0:r, h, :], v_tok[0:r, m, h * 512:(h + 1) * 512]))
                    ch.step(nc.vector.bn_aggr(mv[0:r, m, :], stats[0:r, :, :].rearrange("p a b -> p (a b)")))
                ch.step(nc.vector.tensor_copy(ss[:], mv[:, :, 1]))
                rsqrt_steps(nc, ch, ss[:], rstd[:], tmp[:], 1.0)
                for m in range(TILES):
                    r = rows(m)
                    ch.step(nc.vector.scalar_tensor_tensor(out=v_tok[0:r, m, :], in0=v_tok[0:r, m, :], scalar=mv[0:r, m, 0:1],
                                                           in1=lng[0:r, :], op0=ALU.subtract, op1=ALU.mult))
                    nc.vector.scalar_tensor_tensor(out=v_tok[0:r, m, :], in0=v_tok[0:r, m, :], scalar=rstd[0:r, m:m + 1],
                                                   in1=lnb[0:r, :], op0=ALU.mult, op1=ALU.add).then_inc(s("v_normed"), 1)


def phase_gating(nc, a, o, ident, par, v_tok, yaT, u_dram, rf, rf_size):
    with ExitStack() as ctx:
        s = Sems(nc, ctx, "p2")
        f = Place(nc, rf, rf_size)
        ws = f("w_s_rows", [P, GROUPS, P])
        wsT = f("w_s_turned", [P, GROUPS, P])
        u = f("u_tok", [P, 2, D])
        ya = f("ya_tok", [P, 2, D])
        psM = ctx.enter_context(nc.psum_tensor("p2_psM", [P, 2, D], F32))
        psT = ctx.enter_context(nc.psum_tensor("p2_psT", [P, 2, KT, P], F32))
        with nc.Block() as block:

            @block.sync
            def _(sp):
                sp.dma_start(ws[:], a["w_s"][0].rearrange("g t s -> t g s")).then_inc(s("ws_ready"), 16)
                for m in range(TILES):
                    if m >= 2:
                        sp.wait_ge(s("ya_ready"), m - 1)
                    sp.dma_start(u[0:rows(m), m % 2, :], u_dram[m * P:m * P + rows(m), :]).then_inc(s(f"u_ready{m % 2}"), 16)

            @block.gpsimd
            def _(pool):
                pool.wait_ge(s("ws_ready"), 16)
                nc.gpsimd.affine_select(out=ws[:], in_=ws[:], compare_op=ALU.is_ge, fill=0.0, base=0,
                                        pattern=[[0, GROUPS], [-1, P]], channel_multiplier=1).then_inc(s("ws_masked"), 1)

            @block.tensor
            def _(pe):
                pe.wait_ge(s("ws_masked"), 1)
                for g in range(GROUPS):
                    last = nc.tensor.transpose(psT[:, 0, g, :], ws[:, g, :], ident[:, :])
                last.then_inc(s("ws_turned"), 1)
                pe.wait_ge(s("wsT_ready"), 1)

                def mix(m):
                    r = rows(m)
                    if m >= 2:
                        pe.wait_ge(s("ya_ready"), m - 1)
                    for g in range(GROUPS):
                        last = nc.tensor.matmul(psM[0:r, m % 2, g * P:(g + 1) * P], wsT[0:r, g, 0:r],
                                                v_tok[0:r, m, g * P:(g + 1) * P], start=True, stop=True)
                    last.then_inc(s("mixed"), 1)

                mix(0)
                for m in range(TILES):
                    if m + 1 < TILES:
                        mix(m + 1)
                    pe.wait_ge(s("ya_ready"), m + 1)
                    if m >= 2:
                        pe.wait_ge(s("yaT_lo"), m - 1)
                    for k in range(KT):
                        last = nc.tensor.transpose(psT[:, m % 2, k, 0:rows(m)], ya[0:rows(m), m % 2, k * P:(k + 1) * P],
                                                   ident[0:rows(m), 0:rows(m)])
                    last.then_inc(s("ya_turned"), 1)

            @block.scalar
            def _(act):
                act.wait_ge(s("ws_turned"), 1)
                nc.scalar.activation(wsT[:], psT[:, 0], ACT.Copy).then_inc(s("wsT_ready"), 1)
                for m in range(TILES):
                    act.wait_ge(s("ya_turned"), m + 1)
                    nc.scalar.activation(yaT[0][:, :, col(m):col(m) + rows(m)], psT[:, m % 2, :, 0:rows(m)],
                                         ACT.Copy).then_inc(s("yaT_hi"), 1)

            @block.vector
            def _(dve):
                clear_gaps(nc, nc.vector, *yaT).then_inc(s("gaps"), 1)

                def lo(m):
                    c = slice(col(m), col(m) + rows(m))
                    dve.wait_ge(s("yaT_hi"), m + 1)
                    nc.vector.tensor_tensor(yaT[1][:, :, c], psT[:, m % 2, :, 0:rows(m)], yaT[0][:, :, c].bitcast(F32),
                                            ALU.subtract).then_inc(s("yaT_lo"), 1)

                for m in range(TILES):
                    r = rows(m)
                    dve.wait_ge(s("mixed"), m + 1)
                    if m >= 2:
                        dve.wait_ge(s("ya_turned"), m - 1)
                    bias = par[0:r, PAR["b_s"]:PAR["b_s"] + GROUPS].unsqueeze(2).to_broadcast([r, GROUPS, P])
                    nc.vector.tensor_tensor(ya[0:r, m % 2, :].rearrange("p (g c) -> p g c", g=GROUPS),
                                            psM[0:r, m % 2, :].rearrange("p (g c) -> p g c", g=GROUPS), bias,
                                            ALU.add).then_inc(s("biased"), 1)
                    dve.wait_ge(s("biased"), m + 1)
                    dve.wait_ge(s(f"u_ready{m % 2}"), 16 * (m // 2 + 1))
                    nc.vector.tensor_tensor(ya[0:r, m % 2, :], ya[0:r, m % 2, :], u[0:r, m % 2, :],
                                            ALU.mult).then_inc(s("ya_ready"), 1)
                    if m >= 1:
                        lo(m - 1)
                lo(TILES - 1)


def feature_product(nc, pe, out, ring, slot, act_pair):
    for ch in range(NCH):
        c = slice(ch * CH, (ch + 1) * CH)
        for k in range(KT):
            w = slice(k * P, (k + 1) * P)
            last = three_passes(nc, out[:, ch, 0:CH], ring.hi[:, slot, w], ring.lo[:, slot, w],
                                act_pair[0][:, k, c], act_pair[1][:, k, c], k == 0, k == KT - 1)
    return last


def by_chunks(t):
    return t.rearrange("p (n c) -> p n c", n=NCH)


def phase_gates(nc, a, par, hT, yaT, ta_dram, gb_dram, rf, rf_size):
    w_gate = a["w_gate"][0].rearrange("(k p) c -> p k c", p=P)
    w_a = a["w_branch_a"][0].rearrange("(k p) c -> p k c", p=P)
    with ExitStack() as ctx:
        s = Sems(nc, ctx, "p3")
        f = Place(nc, rf, rf_size)
        ring = Weights(nc, s, "p3", 6, f, f)
        ga = f("g_a", [P, COLS])
        gb = f("g_b", [P, COLS])
        ps = ctx.enter_context(nc.psum_tensor("p3_ps", [P, 2, 4, 512], F32))
        with nc.Block() as block:

            @block.sync
            def _(sp):
                with sp.Fori(0, KT // 2) as i:
                    for n in range(6):
                        kind, j = n % 3, i * 2 * P + (n // 3) * P
                        src = w_a[:, :, bass.ds(j, P)] if kind == 2 else w_gate[:, :, bass.ds(j + kind * D, P)]
                        ring.load(sp, i * 6 + n, n % 2, src, KT)

            @block.gpsimd
            def _(pool):
                ring.start_pool(pool)
                with pool.Fori(0, KT // 2) as i:
                    for n in range(6):
                        pool.wait_ge(s("product"), i * 6 + (n + 1))
                        ring.split_one(pool, i * 6 + n, i * 3 + n // 2, n, n % 2)

            @block.tensor
            def _(pe):
                pe.sem_inc(s("product"), 6)
                with pe.Fori(0, KT // 2) as i:
                    for n in range(6):
                        ring.ready(pe, i * 6 + n)
                        pe.wait_ge(s("ps_free"), i * 6 + n + 1)
                        last = feature_product(nc, pe, ps[:, n % 2], ring, n, yaT if n % 3 == 2 else hT)
                        last.then_inc(s("product"), 1)

            @block.scalar
            def _(act):
                act.sem_inc(s("ta_stored"), 16)
                act.sem_inc(s("gb_stored"), 16)
                with act.Fori(0, KT // 2) as i:
                    for u in range(2):
                        act.wait_ge(s("product"), i * 6 + (3 * u + 7))
                        act.wait_ge(s("ta_stored"), (i * 2 + (u + 1)) * 16)
                        nc.scalar.activation(by_chunks(ga[:, :]), ps[:, (3 * u) % 2, 0:NCH, 0:CH], ACT.Sigmoid,
                                             bias=par[:, bass.ds(i * 2 + (PAR["b_gate"] + u), 1)]).then_inc(s("gate"), 1)
                        act.wait_ge(s("product"), i * 6 + (3 * u + 8))
                        act.wait_ge(s("gb_stored"), (i * 2 + (u + 1)) * 16)
                        nc.scalar.activation(by_chunks(gb[:, :]), ps[:, (3 * u + 1) % 2, 0:NCH, 0:CH], ACT.Sigmoid,
                                             bias=par[:, bass.ds(i * 2 + (PAR["b_gate"] + KT + u), 1)]).then_inc(s("gate"), 1)
                        act.wait_ge(s("gate"), i * 4 + (2 * u + 2))
                        act.dma_start(gb_dram[bass.ds(i * 2 + u, 1), :, :].rearrange("o p c -> (o p) c"), gb[:, :]).then_inc(s("gb_stored"), 16)
                        act.wait_ge(s("ta_ready"), i * 2 + (u + 1))
                        act.dma_start(ta_dram[bass.ds(i * 2 + u, 1), :, :].rearrange("o p c -> (o p) c"), ga[:, :]).then_inc(s("ta_stored"), 16)
                act.wait_ge(s("ta_stored"), 16 * (KT + 1))
                act.wait_ge(s("gb_stored"), 16 * (KT + 1))

            @block.vector
            def _(dve):
                dve.sem_inc(s("ps_free"), 2)
                with dve.Fori(0, KT // 2) as i:
                    for u in range(2):
                        dve.wait_ge(s("gate"), i * 4 + (2 * u + 1))
                        nc.vector.sem_inc(s("ps_free"), 1)
                        dve.wait_ge(s("gate"), i * 4 + (2 * u + 2))
                        nc.vector.sem_inc(s("ps_free"), 1)
                        dve.wait_ge(s("product"), i * 6 + (3 * u + 9))
                        nc.vector.tensor_tensor(by_chunks(ga[:, :]), ps[:, (3 * u + 2) % 2, 0:NCH, 0:CH],
                                                by_chunks(ga[:, :]), ALU.mult).then_inc(s("ta_ready"), 1)
                        dve.wait_ge(s("ta_ready"), i * 2 + (u + 1))
                        nc.vector.sem_inc(s("ps_free"), 1)


def phase_prompt_attention(nc, o, ident, ybT, q_dram, start, size):
    QT = SEQ // P
    STEPS = 2 * QT
    k_rows = o["new_sb_k_prompt"][0, 0].rearrange("(n p) h d -> p n (h d)", p=P)
    v_rows = o["new_sb_v_prompt"][0, 0].rearrange("(n p) h d -> p n (h d)", p=P)
    q_rows = q_dram[0:SEQ, :].rearrange("(n p) c -> p n c", p=P)
    half = KT // 2
    with ExitStack() as ctx:
        s = Sems(nc, ctx, "p4")
        f = Place(nc, start, size)
        raw_k = f("p4_raw_k", [P, QT, P])
        raw_q = f("p4_raw_q", [P, QT, P])
        raw_v = f("p4_raw_v", [P, QT, P])
        twice = f("p4_twice", [P, 2, QT, 2, DH])
        kT_hi = f("p4_kT_hi", [P, 2, SEQ], F32R)
        kT_lo = f("p4_kT_lo", [P, 2, SEQ], F32R)
        qT = f("p4_qT", [P, 2, SEQ], F32R)
        v2 = f("p4_v", [P, 2, QT, 2, DH], F32R)
        nb = f("p4_one_minus_beta", [P, 2, SEQ])
        rest = f("p4_rest", [P, 2, SEQ])
        wt = f("p4_weights", [P, 4, SEQ])
        aT = f("p4_aT", [P, 2, QT, 2, P], F32R)
        ytmp = f("p4_ytmp", [64, 2, 256])
        ysum = f("p4_ysum", [64, 2, 256])
        yb = f("p4_yb", [P, SEQ])
        psZ = ctx.enter_context(nc.psum_tensor("p4_psZ", [P, 2, SEQ], F32))
        psT = ctx.enter_context(nc.psum_tensor("p4_psT", [P, 2, 4, P], F32))
        psY = ctx.enter_context(nc.psum_tensor("p4_psY", [P, 512], F32))
        psP = ctx.enter_context(nc.psum_tensor("p4_psP", [P, 4, P], F32))

        def groups_before(u):
            return sum(1 if (x % QT) < 4 else 2 for x in range(u))

        NG = groups_before(STEPS)

        def lagged(u, lag):
            return (u - lag) % STEPS, (u - lag) < 0

        def bodies(eng, body, tail):
            body(0, True, False)
            with eng.Fori(1, PAIRS - 1) as p:
                body(p, False, False)
            body(PAIRS - 1, False, True)
            tail()

        def prep_piece(u):
            if 3 <= u < 7:
                return u - 3, 1
            if 11 <= u < 15:
                return u - 11, 0
            return None

        with nc.Block() as block:

            @block.sync
            def _(sp):
                def load(p, after):
                    c = bass.ds(p * P, P)
                    if after is not None:
                        sp.wait_ge(s("doubled"), after * 4 + 4)
                        sp.wait_ge(s("v_split"), after * 4 + 4)
                    sp.dma_start(raw_k[:], k_rows[:, :, c]).then_inc(s("raw_k"), 16)
                    sp.dma_start(raw_q[:], q_rows[:, :, c]).then_inc(s("raw_q"), 16)
                    sp.dma_start(raw_v[:], v_rows[:, :, c]).then_inc(s("raw_v"), 16)

                load(0, None)
                with sp.Fori(1, PAIRS) as p:
                    load(p, p - 1)

            @block.tensor
            def _(pe):
                def turn_piece(h, piece, parity):
                    which, g = piece // 2, piece % 2
                    pe.wait_ge(s("doubled"), h * 2 + (which + 1))
                    pe.wait_ge(s("prep_lo"), h * 4 + (piece + 1))
                    for t in range(4):
                        last = nc.tensor.transpose(psP[:, t, :], twice[:, which, 4 * g + t].rearrange("p a d -> p (a d)"),
                                                   ident[:, :])
                    last.then_inc(s("prep_turned"), 1)

                def z(p, u):
                    i, par = u % QT, u // QT
                    h = p * 2 + par
                    pe.wait_ge(s("prep_lo"), h * 4 + 5)
                    pe.wait_ge(s("beta"), p * STEPS + (u + 1))
                    keys = (i + 1) * P
                    for c in range(0, keys, 512):
                        n = max(min(512, keys - c), 256)
                        stat = qT[:, par, i * P:(i + 1) * P]
                        nc.tensor.matmul(psZ[:, u % 2, c:c + n], stat, kT_lo[:, par, c:c + n], start=True, stop=False)
                        last = nc.tensor.matmul(psZ[:, u % 2, c:c + n], stat, kT_hi[:, par, c:c + n], start=False, stop=True)
                    last.then_inc(s("z"), 1)

                def turn(p, u):
                    i = u % QT
                    pe.wait_ge(s("weights"), p * STEPS + (u + 3))
                    g0 = groups_before(u)
                    for g in range((i + 4) // 4):
                        pe.wait_ge(s("aT_lo"), p * NG + (g0 + g + 1))
                        for t in range(4 * g, min(4 * g + 4, i + 1)):
                            last = nc.tensor.transpose(psT[:, (g0 + g) % 2, t % 4, :], wt[:, u % 4, t * P:(t + 1) * P],
                                                       ident[:, :])
                        last.then_inc(s("turned"), 1)

                def av(p, u):
                    i, par = u % QT, u // QT
                    g1 = groups_before(u + 1)
                    pe.wait_ge(s("aT_lo"), p * NG + (g1 + 2))
                    pe.wait_ge(s("v_split"), p * 4 + (2 * par + 2))
                    pe.wait_ge(s("y_first"), p * STEPS + (u + 1))
                    for t in range(i + 1):
                        last = nc.tensor.matmul(psY[:, 0:256], v2[:, par, t].rearrange("p a d -> p (a d)"),
                                                aT[:, u % 2, t].rearrange("p a q -> p (a q)"), start=(t == 0), stop=(t == i))
                    last.then_inc(s("av"), 1)

                def body(p, first, last):
                    for u in range(STEPS):
                        z(p, u)
                        v, old = lagged(u, 2)
                        if not (old and first):
                            turn(p - 1 if old else p, v)
                        piece = prep_piece(u)
                        if piece and not (last and piece[1] == 0):
                            turn_piece(p * 2 + (1 if piece[1] else 2), *piece)
                        v, old = lagged(u, 3)
                        if not (old and first):
                            av(p - 1 if old else p, v)

                def tail():
                    turn(PAIRS - 1, STEPS - 2)
                    av(PAIRS - 1, STEPS - 3)
                    turn(PAIRS - 1, STEPS - 1)
                    av(PAIRS - 1, STEPS - 2)
                    av(PAIRS - 1, STEPS - 1)

                pe.sem_inc(s("av"), 2)
                for piece in range(4):
                    turn_piece(0, piece, 0)
                bodies(pe, body, tail)

            @block.scalar
            def _(act):
                def prep_hi(h, piece, par):
                    which, g = piece // 2, piece % 2
                    act.wait_ge(s("prep_turned"), h * 4 + (piece + 1))
                    dst = (qT if which else kT_hi)[:, par, 512 * g:512 * g + 512]
                    nc.scalar.activation(dst, psP[:].rearrange("p t c -> p (t c)"), ACT.Copy).then_inc(s("prep_hi"), 1)

                def sigmoids(p, u):
                    n = (u % QT + 1) * P
                    act.wait_ge(s("z"), p * STEPS + (u + 1))
                    act.wait_ge(s("scanned"), p * STEPS + (u + 1))
                    nc.scalar.activation(nb[:, u % 2, 0:n], psZ[:, u % 2, 0:n], ACT.Sigmoid, scale=-SCALE).then_inc(s("nb"), 1)
                    nc.scalar.activation(wt[:, u % 4, 0:n], psZ[:, u % 2, 0:n], ACT.Sigmoid, scale=SCALE).then_inc(s("beta"), 1)

                def split_hi(p, u):
                    i = u % QT
                    g0 = groups_before(u)
                    act.wait_ge(s("av"), p * STEPS + (u + 1))
                    for g in range((i + 4) // 4):
                        n = min(4, i + 1 - 4 * g)
                        act.wait_ge(s("turned"), p * NG + (g0 + g + 1))
                        nc.scalar.activation(aT[:, u % 2, 4 * g:4 * g + n, 0, :], psT[:, (g0 + g) % 2, 0:n, :],
                                             ACT.Copy).then_inc(s("aT_hi"), 1)

                def y_low_rows(p, u):
                    act.wait_ge(s("av"), p * STEPS + (u + 3))
                    nc.scalar.activation(ytmp[:, u % 2, :], psY[64:128, 0:256], ACT.Copy).then_inc(s("y_low"), 1)

                def y_hi(p):
                    act.wait_ge(s("y"), (p + 1) * STEPS)
                    nc.scalar.activation(ybT[0][:, bass.ds(p, 1), GAP:GAP + SEQ].rearrange("p o c -> p (o c)"), yb[:, :],
                                         ACT.Copy).then_inc(s("yb_hi"), 1)

                def body(p, first, last):
                    for u in range(STEPS):
                        sigmoids(p, u)
                        v, old = lagged(u, 2)
                        if not (old and first):
                            split_hi(p - 1 if old else p, v)
                        piece = prep_piece(u)
                        if piece and not (last and piece[1] == 0):
                            prep_hi(p * 2 + (1 if piece[1] else 2), *piece)
                        v, old = lagged(u, 3)
                        if not (old and first):
                            y_low_rows(p - 1 if old else p, v)
                            if v == STEPS - 1:
                                y_hi(p - 1)

                def tail():
                    q = PAIRS - 1
                    split_hi(q, STEPS - 2)
                    y_low_rows(q, STEPS - 3)
                    split_hi(q, STEPS - 1)
                    y_low_rows(q, STEPS - 2)
                    y_low_rows(q, STEPS - 1)
                    y_hi(q)

                act.sem_inc(s("beta"), 2)
                for piece in range(4):
                    prep_hi(0, piece, 0)
                bodies(act, body, tail)

            @block.gpsimd
            def _(pool):
                def split_v(h, p, par, after):
                    pool.wait_ge(s("raw_v"), p * 16 + 16)
                    if after is not None:
                        pool.wait_ge(s("av"), after + 2)
                        hold(pool, s("pool_passed"))
                    src = raw_v[:, :, par * DH:(par + 1) * DH]
                    nc.gpsimd.tensor_scalar(v2[:, par, :, 0, :], src, 1.0, 0.0, ALU.mult, ALU.add).then_inc(s("v_split"), 1)
                    pool.wait_ge(s("v_split"), h * 2 + 1)
                    nc.gpsimd.tensor_tensor(v2[:, par, :, 1, :], src, v2[:, par, :, 0, :].bitcast(F32),
                                            ALU.subtract).then_inc(s("v_split"), 1)

                def masks(p, u):
                    d = slice((u % QT) * P, (u % QT + 1) * P)
                    pool.wait_ge(s("nb"), p * STEPS + (u + 1))
                    hold(pool, s("pool_passed"))
                    nc.gpsimd.affine_select(out=nb[:, u % 2, d], in_=nb[:, u % 2, d], compare_op=ALU.is_gt, fill=1.0,
                                            base=0, pattern=[[-1, P]], channel_multiplier=1).then_inc(s("nb_masked"), 1)
                    pool.wait_ge(s("beta"), p * STEPS + (u + 3))
                    hold(pool, s("pool_passed"))
                    nc.gpsimd.affine_select(out=wt[:, u % 4, d], in_=wt[:, u % 4, d], compare_op=ALU.is_gt, fill=0.0,
                                            base=0, pattern=[[-1, P]], channel_multiplier=1).then_inc(s("beta_masked"), 1)

                def weigh(p, u):
                    n = (u % QT + 1) * P
                    pool.wait_ge(s("scanned"), p * STEPS + (u + 3))
                    pool.wait_ge(s("beta_masked"), p * STEPS + (u + 1))
                    nc.gpsimd.tensor_tensor(wt[:, u % 4, 0:n - 1], wt[:, u % 4, 0:n - 1], rest[:, u % 2, 1:n],
                                            ALU.mult).then_inc(s("weights"), 1)

                def body(p, first, last):
                    for u in range(STEPS):
                        masks(p, u)
                        v, old = lagged(u, 1)
                        if not (old and first):
                            weigh(p - 1 if old else p, v)
                        if u == 4:
                            split_v(p * 2 + 1, p, 1, p * STEPS)
                        if u == 12 and not last:
                            split_v(p * 2 + 2, p + 1, 0, p * STEPS + QT)

                pool.sem_inc(s("weights"), 2)
                split_v(0, 0, 0, None)
                bodies(pool, body, lambda: weigh(PAIRS - 1, STEPS - 1))

            @block.vector
            def _(dve):
                def double(h, p, which, par, first=False):
                    dve.wait_ge(s("raw_q" if which else "raw_k"), p * 16 + 16)
                    if not first:
                        dve.wait_ge(s("prep_turned"), h * 4 - 4 + (2 * which + 2))
                    src = (raw_q if which else raw_k)[:, :, par * DH:(par + 1) * DH]
                    nc.vector.tensor_copy(twice[:, which], src.unsqueeze(2).to_broadcast([P, QT, 2, DH])).then_inc(s("doubled"), 1)

                def prep_lo(h, piece, par):
                    which, g = piece // 2, piece % 2
                    dve.wait_ge(s("prep_hi"), h * 4 + (piece + 1))
                    c = slice(512 * g, 512 * g + 512)
                    flat = psP[:].rearrange("p t c -> p (t c)")
                    if which:
                        nc.vector.tensor_tensor(qT[64:128, par, c], flat[64:128, :], qT[64:128, par, c].bitcast(F32),
                                                ALU.subtract).then_inc(s("prep_lo"), 1)
                    else:
                        nc.vector.tensor_tensor(kT_lo[:, par, c], flat, kT_hi[:, par, c].bitcast(F32),
                                                ALU.subtract).then_inc(s("prep_lo"), 1)

                def scan(p, u):
                    n = (u % QT + 1) * P
                    dve.wait_ge(s("nb_masked"), p * STEPS + (u + 1))
                    dve.wait_ge(s("weights"), p * STEPS + (u + 1))
                    src = nb[:, u % 2, n - 1::-1]
                    nc.vector.tensor_tensor_scan(rest[:, u % 2, n - 1::-1], src, src, 1.0, ALU.mult,
                                                 ALU.bypass).then_inc(s("scanned"), 1)

                def split_lo(p, u):
                    i, g0 = u % QT, groups_before(u)
                    for g in range((i + 4) // 4):
                        n = min(4, i + 1 - 4 * g)
                        dve.wait_ge(s("aT_hi"), p * NG + (g0 + g + 1))
                        t = slice(4 * g, 4 * g + n)
                        nc.vector.tensor_tensor(aT[:, u % 2, t, 1, :], psT[:, (g0 + g) % 2, 0:n, :],
                                                aT[:, u % 2, t, 0, :].bitcast(F32), ALU.subtract).then_inc(s("aT_lo"), 1)

                def y_sum(p, u, wait_yb):
                    i, par = u % QT, u // QT
                    dve.wait_ge(s("y_low"), p * STEPS + (u + 1))
                    nc.vector.tensor_tensor(ysum[:, u % 2, :], psY[0:64, 0:256], ytmp[:, u % 2, :], ALU.add).then_inc(s("y_first"), 1)
                    dve.wait_ge(s("y_first"), p * STEPS + (u + 2))
                    if wait_yb:
                        dve.wait_ge(s("yb_hi"), p)
                        dve.wait_ge(s("yb_lo"), p)
                    nc.vector.tensor_tensor(yb[64 * par:64 * par + 64, i * P:(i + 1) * P], ysum[:, u % 2, 0:P],
                                            ysum[:, u % 2, P:2 * P], ALU.add).then_inc(s("y"), 1)

                def y_lo(p):
                    dve.wait_ge(s("yb_hi"), p + 1)
                    pair = bass.ds(p, 1)
                    nc.vector.tensor_tensor(ybT[1][:, pair, GAP:GAP + SEQ].rearrange("p o c -> p (o c)"), yb[:, :],
                                            ybT[0][:, pair, GAP:GAP + SEQ].rearrange("p o c -> p (o c)").bitcast(F32),
                                            ALU.subtract).then_inc(s("yb_lo"), 1)

                def body(p, first, last):
                    for u in range(STEPS):
                        scan(p, u)
                        v, old = lagged(u, 2)
                        if not (old and first):
                            split_lo(p - 1 if old else p, v)
                        if u in (1, 2):
                            double(p * 2 + 1, p, u - 1, 1)
                        if u in (9, 10) and not last:
                            double(p * 2 + 2, p + 1, u - 9, 0)
                        piece = prep_piece(u)
                        if piece and not (last and piece[1] == 0):
                            prep_lo(p * 2 + (1 if piece[1] else 2), *piece)
                        v, old = lagged(u, 3)
                        if not (old and first):
                            y_sum(p - 1 if old else p, v, v == 0 and not first)
                            if v == STEPS - 1:
                                y_lo(p - 1)

                def tail():
                    q = PAIRS - 1
                    split_lo(q, STEPS - 2)
                    y_sum(q, STEPS - 3, False)
                    split_lo(q, STEPS - 1)
                    y_sum(q, STEPS - 2, False)
                    y_sum(q, STEPS - 1, False)
                    y_lo(q)

                dve.sem_inc(s("prep_lo"), 1)
                dve.sem_inc(s("scanned"), 2)
                dve.sem_inc(s("aT_lo"), 2)
                dve.sem_inc(s("y_first"), 1)
                clear_gaps(nc, nc.vector, *ybT).then_inc(s("gaps"), 1)
                double(0, 0, 0, 0, True)
                double(0, 0, 1, 0, True)
                for piece in range(4):
                    prep_lo(0, piece, 0)
                bodies(dve, body, tail)


def phase_sample_attention(nc, a, o, ident, ybT, q_dram, start, size):
    KEYS = PAST + DEC
    TK = PAST // P + 1
    GR = [(0, 4), (4, 8), (8, 12), (12, 16), (16, 17)]
    G = len(GR)
    ITEMS = [("A", 0), ("A", 1), ("K", 0), ("A", 2), ("K", 1), ("A", 3), ("K", 2), ("A", 4), ("K", 3), ("K", 4)]
    BANKS = 3
    ZG = [(0, 1024, (512, 512)), (1024, 800, (512, 288)), (1824, 288, (288,))]
    caches = [(a["cache_sb_k"][0, 0].rearrange("(n p) h d -> p n (h d)", p=P),
               o["new_sb_k_sample"][0, 0].rearrange("t h d -> t (h d)")),
              (a["cache_sb_v"][0, 0].rearrange("(n p) h d -> p n (h d)", p=P),
               o["new_sb_v_sample"][0, 0].rearrange("t h d -> t (h d)"))]
    with ExitStack() as ctx:
        s = Sems(nc, ctx, "p5")
        f = Place(nc, start, size)
        raw_k = f("p5_raw_k", [P, 2, TK, P])
        raw_v = f("p5_raw_v", [P, TK, P])
        raw_q = f("p5_raw_q", [64, 2, P])
        q_hi = f("p5_q_hi", [P, P], F32R)
        q_lo = f("p5_q_lo", [P, P], F32R)
        kT_hi = f("p5_kT_hi", [P, KEYS], F32R)
        kT_lo = f("p5_kT_lo", [P, KEYS], F32R)
        v2 = f("p5_v", [P, 2, TK, 2, P], F32R)
        nb = f("p5_one_minus_beta", [P, KEYS])
        rest = f("p5_rest", [P, KEYS])
        wt = f("p5_weights", [P, 2, KEYS])
        aT = f("p5_aT", [P, TK, 2, P], F32R)
        seen = f("p5_seen", [P, 2, DEC])
        ytmp = f("p5_ytmp", [P, P])
        yb = f("p5_yb", [P, DEC])
        psZ = ctx.enter_context(nc.psum_tensor("p5_psZ", [P, 2, 1024], F32))
        psR = ctx.enter_context(nc.psum_tensor("p5_psR", [P, BANKS, 4, P], F32))
        psY = ctx.enter_context(nc.psum_tensor("p5_psY", [P, 512], F32))
        QCOL = P

        def bodies(eng, step):
            step(-1, 1)
            step(0, 0)
            with eng.Fori(0, 3) as i:
                step(i * 2 + 1, 1)
                step(i * 2 + 2, 0)
            step(PAIRS - 1, 1)
            step(PAIRS, 0)

        def fixed(t):
            return isinstance(t, int)

        def has_z(t):
            return not fixed(t) or 0 <= t < PAIRS

        def has(t, kind):
            pair = t + 1 if kind == "K" else t - 1 if fixed(t) else 0
            return not fixed(t) or 0 <= pair < PAIRS

        def count(t, kind, g):
            return t * G + (G + g + 1) if kind == "K" else t * G + (g + 1 - G)

        with nc.Block() as block:

            @block.sync
            def _(sp):
                def load(t, b, n):
                    c = bass.ds(t * P, P)
                    dst, sem = ((raw_k[:, b], f"raw_k{b}"), (raw_v, "raw_v"))[n]
                    past, new = caches[n]
                    sp.dma_start(dst[:, 0:TK - 1, :], past[:, :, c]).then_inc(s(sem), 16)
                    sp.dma_start(dst[0:DEC, TK - 1, :], new[:, c]).then_inc(s(sem), 16)
                    if not n:
                        sp.dma_start(raw_q[:, b, :], q_dram[SEQ:SEQ + DEC, c]).then_inc(s(sem), 16)

                def load_v(t, b):
                    sp.wait_ge(s("v_split"), t * 2 + 2)
                    load(t, b, 1)

                load(0, 0, 0)
                load(1, 1, 0)
                load_v(0, 0)
                with sp.Fori(0, 3) as i:
                    for n in (1, 2):
                        t = i * 2 + n
                        sp.wait_ge(s("K_turned"), t * G)
                        load(t + 1, (n + 1) % 2, 0)
                        load_v(t, n % 2)
                load_v(PAIRS - 1, 1)

            @block.tensor
            def _(pe):
                def bank_free(t, i):
                    before = [(t - 1, j) for j in range(len(ITEMS))] + [(t, j) for j in range(i)]
                    for at, j in reversed(before):
                        if j % BANKS == i % BANKS and has(at, ITEMS[j][0]) and (fixed(t) or i >= BANKS or ITEMS[j][0] == "K"):
                            kind, g = ITEMS[j]
                            pe.wait_ge(s(f"{kind}_lo"), count(at, kind, g) + (G if kind == "A" else 0))
                            break
                    if i == 1 and not fixed(t):
                        pe.wait_ge(s("A_lo"), count(t - 1, "A", G - 1) + G)

                def item(t, b, i):
                    kind, g = ITEMS[i]
                    if not has(t, kind):
                        return
                    bank_free(t, i)
                    hold(pe, s("pe_passed"))
                    if kind == "K":
                        for k in range(*GR[g]):
                            r = P if k < TK - 1 else DEC
                            last = nc.tensor.transpose(psR[:, i % BANKS, k % 4, 0:r], raw_k[0:r, 1 - b, k, :], ident[0:r, 0:r])
                        if g == G - 1:
                            last = nc.tensor.transpose(psR[:, i % BANKS, 1, 0:DEC], raw_q[:, 1 - b, :], ident[0:DEC, 0:DEC])
                    else:
                        for k in range(*GR[g]):
                            r = P if k < TK - 1 else DEC
                            last = nc.tensor.transpose(psR[0:r, i % BANKS, k % 4, :], wt[:, 1 - b, k * P:k * P + r],
                                                       ident[:, :])
                    last.then_inc(s(f"{kind}_turned"), 1)

                def z(t, b, g):
                    if not has_z(t):
                        return
                    c0, _, parts = ZG[g]
                    if g == 0:
                        pe.wait_ge(s("K_lo"), t * G + G)
                    pe.wait_ge(s("beta"), t * 3 + (g + 1))
                    at = 0
                    for n in parts:
                        c, out = slice(c0 + at, c0 + at + n), psZ[:, (3 * b + g) % 2, at:at + n]
                        last = three_passes(nc, out, q_hi[:], q_lo[:], kT_hi[:, c], kT_lo[:, c], True, True)
                        at += n
                    last.then_inc(s("z"), 1)

                def av(t, b):
                    if not has(t, "A"):
                        return
                    pe.wait_ge(s("A_lo"), t * G + G)
                    pe.wait_ge(s("v_split"), t * 2 + 2)
                    pe.wait_ge(s("y_sum"), t * 2)
                    for k in range(TK):
                        r = P if k < TK - 1 else DEC
                        for part in (1, 0):
                            last = nc.tensor.matmul(psY[:, 0:256], v2[0:r, 1 - b, k, part, :],
                                                    aT[0:r, k].rearrange("p a q -> p (a q)"),
                                                    start=(k == 0 and part == 1), stop=(k == TK - 1 and part == 0))
                    last.then_inc(s("av"), 1)

                def step(t, b):
                    if has(t, "K"):
                        pe.wait_ge(s(f"raw_k{1 - b}"), (t * 24 + 72) if b == 1 else (t * 24 + 48))
                    z(t, b, 0)
                    z(t, b, 1)
                    if has(t, "A"):
                        pe.wait_ge(s("weights"), t + 1)
                    item(t, b, 0)
                    item(t, b, 1)
                    z(t, b, 2)
                    for i in range(2, len(ITEMS)):
                        item(t, b, i)
                    av(t, b)

                pe.sem_inc(s("av"), 2)
                bodies(pe, step)

            @block.scalar
            def _(act):
                def item(t, b, i):
                    kind, g = ITEMS[i]
                    if not has(t, kind):
                        return
                    k0, k1 = GR[g]
                    act.wait_ge(s(f"{kind}_turned"), count(t, kind, g))
                    if kind == "K":
                        c0, c1 = k0 * P, min(k1 * P, KEYS)
                        last = nc.scalar.activation(kT_hi[:, c0:c1], psR[:, i % BANKS].rearrange("p t c -> p (t c)")[:, 0:c1 - c0], ACT.Copy)
                        if g == G - 1:
                            for h in (slice(0, 64), slice(64, 128)):
                                last = nc.scalar.activation(q_hi[h, h], psR[h, i % BANKS, 1, 0:DEC], ACT.Copy)
                    else:
                        r = P if k0 < TK - 1 else DEC
                        if g == 0:
                            act.wait_ge(s("av"), t + 1)
                        last = nc.scalar.activation(aT[0:r, k0:k1, 0, :], psR[0:r, i % BANKS, 0:k1 - k0, :], ACT.Copy)
                    last.then_inc(s(f"{kind}_hi"), 1)

                def sigmoids(t, b, g):
                    if not has_z(t):
                        return
                    if g == 0:
                        act.wait_ge(s("scanned"), t + 1)
                    c0, n, _ = ZG[g]
                    act.wait_ge(s("z"), t * 3 + (g + 1))
                    src = psZ[:, (3 * b + g) % 2, 0:n]
                    nc.scalar.activation(nb[:, c0:c0 + n], src, ACT.Sigmoid, scale=-SCALE).then_inc(s("nb"), 1)
                    nc.scalar.activation(wt[:, b, c0:c0 + n], src, ACT.Sigmoid, scale=SCALE).then_inc(s("beta"), 1)

                def step(t, b):
                    sigmoids(t, b, 0)
                    sigmoids(t, b, 1)
                    item(t, b, 0)
                    item(t, b, 1)
                    sigmoids(t, b, 2)
                    for i in range(2, len(ITEMS)):
                        item(t, b, i)
                    if has(t, "A"):
                        act.wait_ge(s("av"), t + 2)
                        nc.scalar.activation(ytmp[:], psY[:, P:2 * P], ACT.Copy).then_inc(s("y_low"), 1)
                        act.wait_ge(s("y_sum"), t * 2 + 2)
                        nc.scalar.activation(ybT[0][:, bass.ds(t - 1, 1), SCOL:COLS].rearrange("p o c -> p (o c)"), yb[:],
                                             ACT.Copy).then_inc(s("yb_hi"), 1)

                act.wait_ge(s("cleared"), 1)
                act.sem_inc(s("beta"), 2)
                bodies(act, step)

            @block.gpsimd
            def _(pool):
                def link(ins):
                    link.n += 1
                    ins.then_inc(s("seen"), 1)
                    pool.wait_ge(s("seen"), link.n)

                link.n = 0
                first_half, second_half = seen[:, 0, :], seen[:, 1, :]
                link(nc.gpsimd.memset(seen[:], 1.0))
                link(nc.gpsimd.affine_select(out=first_half, in_=first_half, compare_op=ALU.is_gt, fill=0.0, base=0,
                                             pattern=[[-1, DEC]], channel_multiplier=1))
                link(nc.gpsimd.affine_select(out=first_half, in_=first_half, compare_op=ALU.is_ge, fill=0.0, base=DEC - 1,
                                             pattern=[[0, DEC]], channel_multiplier=-1))
                link(nc.gpsimd.affine_select(out=second_half, in_=second_half, compare_op=ALU.is_gt, fill=0.0, base=-DEC,
                                             pattern=[[-1, DEC]], channel_multiplier=1))
                link(nc.gpsimd.tensor_tensor(first_half, first_half, second_half, ALU.add))
                link(nc.gpsimd.tensor_scalar(second_half, first_half, -1.0, 1.0, ALU.mult, ALU.add))
                pool.sem_inc(s("v_split"), 2)
                with pool.Fori(0, PAIRS // 2) as i:
                    for b in range(2):
                        t = i * 2 + b
                        pool.wait_ge(s("raw_v"), t * 32 + 32)
                        pool.wait_ge(s("av"), t + 1)
                        hold(pool, s("pool_passed"))
                        for part in range(2):
                            if part:
                                pool.wait_ge(s("v_split"), t * 2 + 3)
                            for k, r in ((slice(0, TK - 1), P), (slice(TK - 1, TK), DEC)):
                                if part:
                                    last = nc.gpsimd.tensor_tensor(v2[0:r, b, k, 1, :], raw_v[0:r, k, :],
                                                                   v2[0:r, b, k, 0, :].bitcast(F32), ALU.subtract)
                                else:
                                    last = nc.gpsimd.tensor_scalar(v2[0:r, b, k, 0, :], raw_v[0:r, k, :], 1.0, 0.0,
                                                                   ALU.mult, ALU.add)
                            last.then_inc(s("v_split"), 1)

            @block.vector
            def _(dve):
                def item(t, b, i):
                    kind, g = ITEMS[i]
                    if not has(t, kind):
                        return
                    k0, k1 = GR[g]
                    dve.wait_ge(s(f"{kind}_hi"), count(t, kind, g))
                    if kind == "K":
                        c0, c1 = k0 * P, min(k1 * P, KEYS)
                        last = nc.vector.tensor_tensor(kT_lo[:, c0:c1], psR[:, i % BANKS].rearrange("p t c -> p (t c)")[:, 0:c1 - c0],
                                                       kT_hi[:, c0:c1].bitcast(F32), ALU.subtract)
                        if g == G - 1:
                            for h in (slice(0, 64), slice(64, 128)):
                                last = nc.vector.tensor_tensor(q_lo[h, h], psR[h, i % BANKS, 1, 0:DEC], q_hi[h, h].bitcast(F32), ALU.subtract)
                    else:
                        r = P if k0 < TK - 1 else DEC
                        last = nc.vector.tensor_tensor(aT[0:r, k0:k1, 1, :], psR[0:r, i % BANKS, 0:k1 - k0, :],
                                                       aT[0:r, k0:k1, 0, :].bitcast(F32), ALU.subtract)
                    last.then_inc(s(f"{kind}_lo"), 1)

                def scan(t, b):
                    new = slice(PAST, KEYS)
                    dve.wait_ge(s("beta"), t * 3 + 5)
                    nc.vector.tensor_tensor(nb[:, new], nb[:, new], seen[:, 1, :], ALU.max).then_inc(s("masked"), 1)
                    nc.vector.tensor_tensor(wt[:, b, new], wt[:, b, new], seen[:, 0, :], ALU.mult).then_inc(s("masked"), 1)
                    dve.wait_ge(s("masked"), t * 2 + 1)
                    dve.wait_ge(s("weights"), t + 1)
                    nc.vector.tensor_tensor_scan(rest[:, ::-1], nb[:, ::-1], nb[:, ::-1], 1.0, ALU.mult,
                                                 ALU.bypass).then_inc(s("scanned"), 1)

                def weigh(t, b):
                    dve.wait_ge(s("masked"), t * 2 + 2)
                    dve.wait_ge(s("scanned"), t + 2)
                    nc.vector.tensor_tensor(wt[:, b, 0:KEYS - 1], wt[:, b, 0:KEYS - 1], rest[:, 1:KEYS],
                                            ALU.mult).then_inc(s("weights"), 1)

                def step(t, b):
                    item(t, b, 0)
                    item(t, b, 1)
                    if has_z(t):
                        scan(t, b)
                    for i in range(2, len(ITEMS)):
                        item(t, b, i)
                        if i == 4 and has_z(t):
                            weigh(t, b)
                    if has(t, "A"):
                        dve.wait_ge(s("y_low"), t)
                        for h in (slice(0, 64), slice(64, 128)):
                            nc.vector.tensor_tensor(yb[h, :], psY[h, h], ytmp[h, h], ALU.add).then_inc(s("y_sum"), 1)
                        dve.wait_ge(s("yb_hi"), t)
                        nc.vector.tensor_tensor(ybT[1][:, bass.ds(t - 1, 1), SCOL:COLS].rearrange("p o c -> p (o c)"), yb[:],
                                                ybT[0][:, bass.ds(t - 1, 1), SCOL:COLS].rearrange("p o c -> p (o c)").bitcast(F32),
                                                ALU.subtract).then_inc(s("yb_lo"), 1)

                dve.wait_ge(s("seen"), 6)
                dve.sem_inc(s("scanned"), 1)
                dve.sem_inc(s("weights"), 1)
                dve.sem_inc(s("A_lo"), G)
                dve.sem_inc(s("y_sum"), 2)
                nc.vector.memset(q_hi[:].bitcast(F32), 0.0)
                nc.vector.memset(q_lo[:].bitcast(F32), 0.0).then_inc(s("cleared"), 1)
                bodies(dve, step)


def phase_merge(nc, a, ybT, mgT, ta_dram, gb_dram, rf, rf_size):
    w_b = a["w_branch_b"][0].rearrange("(k p) c -> p k c", p=P)
    with ExitStack() as ctx:
        s = Sems(nc, ctx, "p6")
        f = Place(nc, rf, rf_size)
        ring = Weights(nc, s, "p6", 4, f, f)
        ta = f("p6_ta", [P, 2, COLS])
        gb = f("p6_gb", [P, 2, COLS])
        ps = ctx.enter_context(nc.psum_tensor("p6_ps", [P, 2, 4, 512], F32))
        U = 4
        with nc.Block() as block:

            @block.sync
            def _(sp):
                with sp.Fori(0, KT // U) as i:
                    for n in range(U):
                        ring.load(sp, i * U + n, n % 2, w_b[:, :, bass.ds(i * U * P + n * P, P)], KT)

            @block.gpsimd
            def _(pool):
                ring.start_pool(pool)
                with pool.Fori(0, KT // U) as i:
                    for n in range(U):
                        pool.wait_ge(s("product"), i * U + (n + 1))
                        ring.split_one(pool, i * U + n, i * 2 + n // 2, n, n % 2)

            @block.tensor
            def _(pe):
                pe.sem_inc(s("product"), U)
                with pe.Fori(0, KT // U) as i:
                    for n in range(U):
                        ring.ready(pe, i * U + n)
                        pe.wait_ge(s("gated"), i * U + (n + 1))
                        feature_product(nc, pe, ps[:, n % 2], ring, n, ybT).then_inc(s("product"), 1)

            @block.scalar
            def _(act):
                act.sem_inc(s("merged_hi"), 2)
                with act.Fori(0, KT // U) as i:
                    for n in range(U):
                        j = i * U + n
                        act.wait_ge(s("merged_lo"), i * U + (n + 1))
                        act.dma_start(ta[:, n % 2, :], ta_dram[bass.ds(j, 1), :, :].rearrange("o p c -> (o p) c")).then_inc(s(f"ta_ready{n % 2}"), 16)
                        act.dma_start(gb[:, n % 2, :], gb_dram[bass.ds(j, 1), :, :].rearrange("o p c -> (o p) c")).then_inc(s(f"gb_ready{n % 2}"), 16)
                        act.wait_ge(s("merged"), i * U + (n + 1))
                        nc.scalar.activation(mgT[0][:, bass.ds(j, 1), GAP:COLS].rearrange("p o c -> p (o c)"), ta[:, n % 2, GAP:COLS],
                                             ACT.Copy).then_inc(s("merged_hi"), 1)

            @block.vector
            def _(dve):
                dve.sem_inc(s("gated"), 2)
                dve.sem_inc(s("merged_lo"), 2)
                with dve.Fori(0, KT // U) as i:
                    for n in range(U):
                        j = i * U + n
                        dve.wait_ge(s("product"), i * U + (n + U + 1))
                        dve.wait_ge(s(f"gb_ready{n % 2}"), (i * (U // 2) + (n // 2 + 1)) * 16)
                        g = by_chunks(gb[:, n % 2, :])
                        nc.vector.tensor_tensor(g, ps[:, n % 2, 0:NCH, 0:CH], g, ALU.mult).then_inc(s("gated"), 1)
                        dve.wait_ge(s("gated"), i * U + (n + 3))
                        dve.wait_ge(s(f"ta_ready{n % 2}"), (i * (U // 2) + (n // 2 + 1)) * 16)
                        nc.vector.tensor_tensor(ta[:, n % 2, :], ta[:, n % 2, :], gb[:, n % 2, :], ALU.add).then_inc(s("merged"), 1)
                        dve.wait_ge(s("merged"), i * U + (n + 1))
                        dve.wait_ge(s("merged_hi"), i * U + (n + 3))
                        nc.vector.tensor_tensor(mgT[1][:, bass.ds(j, 1), GAP:COLS].rearrange("p o c -> p (o c)"), ta[:, n % 2, GAP:COLS],
                                                mgT[0][:, bass.ds(j, 1), GAP:COLS].rearrange("p o c -> p (o c)").bitcast(F32),
                                                ALU.subtract).then_inc(s("merged_lo"), 1)


def phase_output(nc, a, ident, mgT, x2_dram, r0, r0_size, rf, rf_size):
    w_o = a["w_o"][0].rearrange("(k p) c -> p k c", p=P)
    h2T = mgT
    LAG = 2
    with ExitStack() as ctx:
        s = Sems(nc, ctx, "p7")
        f = Place(nc, rf, rf_size)
        ring = Weights(nc, s, "p7", 8, f, Place(nc, r0, r0_size))
        g_post = f("g_post_row", [P, D])
        g_ffn = f("g_ffn_row", [P, D])
        x = f("p7_x", [P, 2, D])
        y = f("p7_y", [P, 2, D])
        h2 = f("p7_h2", [P, 2, D])
        junk = f("p7_squares", [P, D])
        ss = f("p7_ss", [P, 2, 2])
        rstd = f("p7_rstd", [P, 2, 2])
        tmp = f("p7_tmp", [P, 2, 2])
        ps = ctx.enter_context(nc.psum_tensor("p7_ps", [P, 2, D], F32))
        psT = ctx.enter_context(nc.psum_tensor("p7_psT", [P, 2, KT, P], F32))
        with nc.Block() as block:

            @block.sync
            def _(sp):
                for n in range(8):
                    ring.load(sp, n, n % 2, w_o[:, 2 * (n % 4):2 * (n % 4) + 2, (n // 4) * 512:(n // 4 + 1) * 512], 2)
                sp.dma_start(g_post[:], a["g_post_mix"].to_broadcast([P, D])).then_inc(s("g_ready"), 16)
                sp.dma_start(g_ffn[:], a["g_pre_ffn"].to_broadcast([P, D])).then_inc(s("g_ready"), 16)
                for m in range(TILES):
                    if m >= 2:
                        sp.wait_ge(s("x2_ready"), m - 1)
                    src = a["x_prompt"][0, m * P:(m + 1) * P, :] if m < TILES - 1 else a["x_sample"][0]
                    sp.dma_start(x[0:rows(m), m % 2, :], src).then_inc(s(f"x_ready{m % 2}"), 16)

            @block.gpsimd
            def _(pool):
                ring.start_pool(pool)
                for n in range(8):
                    ring.split_one(pool, n, n // 2, n, n % 2)
                for m in range(TILES):
                    pool.wait_ge(s("x2_ready"), m + 1)
                    pool.dma_start(x2_dram[m * P:m * P + rows(m), :], y[0:rows(m), m % 2, :]).then_inc(s(f"x2_stored{m % 2}"), 16)
                pool.wait_ge(s("x2_stored0"), 16 * 5)
                pool.wait_ge(s("x2_stored1"), 16 * 4)

            @block.tensor
            def _(pe):
                def product(m):
                    for c in range(2):
                        if m == 0:
                            ring.ready(pe, 4 * c + 3)
                        if m >= 2 and c == 0:
                            pe.wait_ge(s("y_scaled"), m - 1)
                        for k in range(KT):
                            slot, at = 4 * c + k // 2, (k % 2) * 512
                            last = three_passes(
                                nc, ps[0:rows(m), m % 2, c * 512:(c + 1) * 512], mgT[0][:, k, col(m):col(m) + rows(m)],
                                mgT[1][:, k, col(m):col(m) + rows(m)], ring.hi[:, slot, at:at + 512],
                                ring.lo[:, slot, at:at + 512], k == 0, k == KT - 1)
                    last.then_inc(s("product"), 1)

                def turn(m):
                    pe.wait_ge(s("h2_ready"), m + 1)
                    if m >= 2:
                        pe.wait_ge(s("h2T_lo"), m - 1)
                    for k in range(KT):
                        last = nc.tensor.transpose(psT[:, m % 2, k, 0:rows(m)], h2[0:rows(m), m % 2, k * P:(k + 1) * P],
                                                   ident[0:rows(m), 0:rows(m)])
                    last.then_inc(s("h2_turned"), 1)

                product(0)
                product(1)
                for m in range(TILES):
                    if m + 2 < TILES:
                        product(m + 2)
                    turn(m)

            @block.scalar
            def _(act):
                def hi(m):
                    act.wait_ge(s("h2_turned"), m + 1)
                    nc.scalar.activation(h2T[0][:, :, col(m):col(m) + rows(m)], psT[:, m % 2, :, 0:rows(m)],
                                         ACT.Copy).then_inc(s("h2T_hi"), 1)

                act.wait_ge(s("ss_set"), 1)
                for m in range(TILES):
                    r = rows(m)
                    act.wait_ge(s("product"), m + 1)
                    if m >= 2:
                        act.wait_ge(s("h2_ready"), m - 1)
                    nc.scalar.activation(junk[0:r, :], ps[0:r, m % 2, :], ACT.Square,
                                         accum_out=ss[0:r, m % 2, 0:1]).then_inc(s("squares"), 1)
                    act.wait_ge(s("squares"), 2 * m + 1)
                    if m >= LAG:
                        hi(m - LAG)
                    act.wait_ge(s("x2_ready"), m + 1)
                    nc.scalar.activation(junk[0:r, :], y[0:r, m % 2, :], ACT.Square,
                                         accum_out=ss[0:r, m % 2, 1:2]).then_inc(s("squares"), 1)
                    act.wait_ge(s("squares"), 2 * m + 2)
                for m in range(TILES - LAG, TILES):
                    hi(m)

            @block.vector
            def _(dve):
                ch = Chain(dve, s("dve_chain"))
                nc.vector.memset(ss[:], 1.0).then_inc(s("ss_set"), 1)
                ch.step(clear_gaps(nc, nc.vector, *h2T))
                dve.wait_ge(s("g_ready"), 32)

                def lo(m):
                    c = slice(col(m), col(m) + rows(m))
                    dve.wait_ge(s("h2T_hi"), m + 1)
                    nc.vector.tensor_tensor(h2T[1][:, :, c], psT[:, m % 2, :, 0:rows(m)], h2T[0][:, :, c].bitcast(F32),
                                            ALU.subtract).then_inc(s("h2T_lo"), 1)

                for m in range(TILES):
                    r, b = rows(m), m % 2
                    dve.wait_ge(s("squares"), 2 * m + 1)
                    rsqrt_steps(nc, ch, ss[0:r, b, 0:1], rstd[0:r, b, 0:1], tmp[0:r, b, 0:1], 1.0 / D)
                    if m >= 2:
                        dve.wait_ge(s(f"x2_stored{b}"), 16 * (m // 2))
                    nc.vector.scalar_tensor_tensor(out=y[0:r, b, :], in0=ps[0:r, b, :], scalar=rstd[0:r, b, 0:1],
                                                   in1=g_post[0:r, :], op0=ALU.mult, op1=ALU.mult).then_inc(s("y_scaled"), 1)
                    dve.wait_ge(s("y_scaled"), m + 1)
                    dve.wait_ge(s(f"x_ready{b}"), 16 * (m // 2 + 1))
                    nc.vector.tensor_tensor(y[0:r, b, :], y[0:r, b, :], x[0:r, b, :], ALU.add).then_inc(s("x2_ready"), 1)
                    if m >= LAG:
                        lo(m - LAG)
                    dve.wait_ge(s("squares"), 2 * m + 2)
                    rsqrt_steps(nc, ch, ss[0:r, b, 1:2], rstd[0:r, b, 1:2], tmp[0:r, b, 1:2], 1.0 / D)
                    if m >= 2:
                        dve.wait_ge(s("h2_turned"), m - 1)
                    nc.vector.scalar_tensor_tensor(out=h2[0:r, b, :], in0=y[0:r, b, :], scalar=rstd[0:r, b, 1:2],
                                                   in1=g_ffn[0:r, :], op0=ALU.mult, op1=ALU.mult).then_inc(s("h2_ready"), 1)
                for m in range(TILES - LAG, TILES):
                    lo(m)


def phase_ffn(nc, a, o, ident, par, h2T, x2_dram, r0, r0_size, rf, rf_size):
    w_up = a["w_up"][0].rearrange("(k p) c -> p k c", p=P)
    w_down = a["w_down"][0].rearrange("(f p) c -> f p c", p=P)
    SHARES = 2 * TILES
    LAST = SCOL + DEC
    with ExitStack() as ctx:
        s = Sems(nc, ctx, "p8")
        f_ = Place(nc, rf, rf_size)
        r_ = Place(nc, r0, r0_size)
        ring = Weights(nc, s, "p8", 6, f_, f_)
        acc = r_("p8_acc", [P, TILES, D])
        hid_hi = r_("p8_hid_hi", [P, COLS], F32R)
        hid_lo = r_("p8_hid_lo", [P, COLS], F32R)
        x = [r_("p8_up_gate", [P, COLS]), r_("p8_up_val", [P, COLS])]
        cv = [r_("p8_conv_gate", [P, COLS]), f_("p8_conv_val", [P, COLS])]
        tails = f_("p8_tails", [P, 4, 2 * FT])
        tail_rows = f_("p8_tail_rows", [2 * FT, 4, P])
        ss = r_("p8_ss", [P, TILES])
        rstd = r_("p8_rstd", [P, TILES])
        tmp = r_("p8_tmp", [P, TILES])
        r1 = r0 + r0_size
        x2 = nc.alloc_sbuf_tensor_at("p8_x2", [P, TILES, D], F32, offset=r1)
        g_row = nc.alloc_sbuf_tensor_at("p8_g_row", [P, D], F32, offset=r1 + TILES * D * 4)
        junk = nc.alloc_sbuf_tensor_at("p8_squares", [P, D], F32, offset=r1 + (TILES + 1) * D * 4)
        psU = ctx.enter_context(nc.psum_tensor("p8_psU", [P, 6, 512], F32))
        psD = ctx.enter_context(nc.psum_tensor("p8_psD", [P, 2, 512], F32))
        state = par[:, PAR["state0"]:PAR["state0"] + 4 * FT].rearrange("p (j t) -> p j t", j=2)

        def bodies(eng, step, tail):
            step(0, 0, True)
            step(1, 1, False)
            with eng.Fori(1, FT // 2) as i:
                step(i * 2, 0, False)
                step(i * 2 + 1, 1, False)
            tail(FT - 1, 1)

        with nc.Block() as block:

            @block.sync
            def _(sp):
                def step(f, b, first):
                    for kind in range(3):
                        src = (w_up[:, :, bass.ds(f * P + kind * FF, P)] if kind < 2
                               else w_down[bass.ds(f, 1), :, :].rearrange("o p (k c) -> (o p) k c", k=KT))
                        ring.load(sp, f * 3 + kind, (3 * b + kind) % 2, src, KT)

                bodies(sp, step, lambda f, b: None)
                sp.wait_ge(s("up"), 2 * FT + 4)
                for m in range(TILES):
                    sp.dma_start(x2[0:rows(m), m, :], x2_dram[m * P:m * P + rows(m), :]).then_inc(s("x2_ready"), 16)
                sp.dma_start(g_row[:], a["g_post_ffn"].to_broadcast([P, D])).then_inc(s("x2_ready"), 16)
                sp.wait_ge(s("tail_rows"), 1)
                for j in range(4):
                    dst = o["new_conv_prompt" if j < 2 else "new_conv_sample"][0, 0, j % 2].rearrange("(t c) -> t c", c=P)
                    sp.dma_start(dst, tail_rows[:, j, :]).then_inc(s("stored"), 16)
                for m in range(TILES):
                    sp.wait_ge(s("y_ready"), m + 1)
                    dst = o["y_prompt"][0, m * P:(m + 1) * P, :] if m < TILES - 1 else o["y_sample"][0]
                    sp.dma_start(dst, x2[0:rows(m), m, :]).then_inc(s("stored"), 16)
                sp.wait_ge(s("stored"), 16 * (TILES + 4))

            @block.gpsimd
            def _(pool):
                def step(f, b, first):
                    for kind in range(3):
                        if kind < 2:
                            pool.wait_ge(s("up"), f * 2 + (kind + 1))
                        else:
                            pool.wait_ge(s("share"), f * SHARES + SHARES)
                        n = 3 * b + kind
                        ring.split_one(pool, f * 3 + kind, (f - b) * 3 // 2 + n // 2, n, n % 2)

                ring.start_pool(pool)
                bodies(pool, step, lambda f, b: None)
                for m in range(TILES):
                    pool.wait_ge(s("scaled"), m + 1)
                    nc.gpsimd.tensor_tensor(x2[0:rows(m), m, :], x2[0:rows(m), m, :], acc[0:rows(m), m, :],
                                            ALU.add).then_inc(s("y_ready"), 1)

            @block.tensor
            def _(pe):
                def up(f, b):
                    for kind in range(2):
                        ring.ready(pe, f * 3 + kind)
                        pe.wait_ge(s("up_taken"), f * 2 + (kind + 1))
                        feature_product(nc, pe, psU[:, 3 * kind:3 * kind + 3], ring, 3 * b + kind, h2T).then_inc(s("up"), 1)

                def down(f, b):
                    ring.ready(pe, f * 3 + 2)
                    pe.wait_ge(s("hid_lo"), f + 2)
                    slot = 3 * b + 2
                    for m in range(TILES):
                        r, c = rows(m), slice(col(m), col(m) + rows(m))
                        for h in range(2):
                            n = 2 * m + h
                            pe.wait_ge(s("added"), f * SHARES + (n + 1))
                            w = slice(h * 512, (h + 1) * 512)
                            three_passes(nc, psD[0:r, n % 2, :], hid_hi[:, c], hid_lo[:, c], ring.hi[:, slot, w],
                                         ring.lo[:, slot, w], True, True).then_inc(s("share"), 1)

                def step(f, b, first):
                    up(f, b)
                    if not first:
                        down(f - 1, 1 - b)

                pe.sem_inc(s("up"), 4)
                pe.sem_inc(s("share"), 2 * SHARES)
                bodies(pe, step, down)
                pe.wait_ge(s("up_taken"), 2 * FT + 2)
                pe.wait_ge(s("tails"), 2 * FT)
                for j in range(4):
                    last = nc.tensor.transpose(psU[0:2 * FT, 0, j * P:(j + 1) * P], tails[:, j, :], ident[:, :])
                last.then_inc(s("tails_turned"), 1)

            @block.scalar
            def _(act):
                def step(f, b, first):
                    for kind in range(2):
                        act.wait_ge(s("up"), f * 2 + (kind + 5))
                        act.wait_ge(s("conv"), f * 2 + (kind + 1))
                        nc.scalar.activation(by_chunks(x[kind][:, :]), psU[:, 3 * kind:3 * kind + 3, 0:CH],
                                             ACT.Copy).then_inc(s("up_taken"), 1)
                        act.wait_ge(s("up_taken"), f * 2 + (kind + 3))
                        if kind == 0:
                            act.wait_ge(s("hid_lo"), f + 1)
                        else:
                            act.wait_ge(s("hid"), f + 1)
                        at = kind * FT
                        nc.scalar.activation(cv[kind][:, GAP:COLS], x[kind][:, GAP:COLS], ACT.Identity,
                                             scale=par[:, bass.ds(f + (PAR["w_conv2"] + at), 1)],
                                             bias=par[:, bass.ds(f + (PAR["b_conv"] + at), 1)]).then_inc(s("conv_begun"), 1)
                    act.wait_ge(s("conv"), f * 2 + 3)
                    nc.scalar.activation(cv[0][:, GAP:COLS], cv[0][:, GAP:COLS], ACT.Gelu_apprx_tanh).then_inc(s("gelu"), 1)
                    act.wait_ge(s("hid"), f + 2)
                    nc.scalar.activation(hid_hi[:, GAP:COLS], cv[0][:, GAP:COLS], ACT.Copy).then_inc(s("hid_hi"), 1)

                act.sem_inc(s("up_taken"), 2)
                bodies(act, step, lambda f, b: None)
                act.wait_ge(s("tails_turned"), 1)
                nc.scalar.activation(tail_rows[:], psU[0:2 * FT, 0, :].rearrange("p (j c) -> p j c", j=4), ACT.Copy).then_inc(s("tail_rows"), 1)
                for m in range(TILES):
                    act.wait_ge(s("added"), (FT - 1) * SHARES + (2 * m + 4))
                    nc.scalar.activation(junk[0:rows(m), :], acc[0:rows(m), m, :], ACT.Square,
                                         accum_out=ss[0:rows(m), m:m + 1]).then_inc(s("squares"), 1)
                    act.wait_ge(s("squares"), m + 1)

            @block.vector
            def _(dve):
                def add_share(f):
                    for m in range(TILES):
                        for h in range(2):
                            n, r = 2 * m + h, rows(m)
                            w = slice(h * 512, (h + 1) * 512)
                            dve.wait_ge(s("share"), f * SHARES + (n + 1 + 2 * SHARES))
                            nc.vector.tensor_tensor(acc[0:r, m, w], psD[0:r, n % 2, :], acc[0:r, m, w],
                                                    ALU.add).then_inc(s("added"), 1)

                def convolve(f, kind):
                    at, xk, ck = kind * FT, x[kind], cv[kind]
                    dve.wait_ge(s("conv_begun"), f * 2 + (kind + 1))
                    nc.vector.tensor_copy(tails[:, 0:2, bass.ds(f + at, 1)], xk[:, GAP + SEQ - 2:GAP + SEQ].unsqueeze(2))
                    nc.vector.tensor_copy(tails[:, 2:4, bass.ds(f + at, 1)], xk[:, LAST - 2:LAST].unsqueeze(2)).then_inc(s("tails"), 1)
                    nc.vector.tensor_copy(xk[:, GAP + SEQ:SCOL].unsqueeze(2), state[:, :, bass.ds(f + at, 1)]).then_inc(s("history"), 1)
                    dve.wait_ge(s("history"), f * 2 + (kind + 1))
                    for j in (1, 0):
                        ins = nc.vector.scalar_tensor_tensor(
                            out=ck[:, GAP:COLS], in0=xk[:, j:COLS - GAP + j],
                            scalar=par[:, bass.ds(f + (PAR[f"w_conv{j}"] + at), 1)], in1=ck[:, GAP:COLS],
                            op0=ALU.mult, op1=ALU.add)
                        if j:
                            ins.then_inc(s("conv_half"), 1)
                            dve.wait_ge(s("conv_half"), f * 2 + (kind + 1))
                    ins.then_inc(s("conv"), 1)

                def step(f, b, first):
                    if not first:
                        add_share(f - 1)
                    convolve(f, 0)
                    convolve(f, 1)
                    dve.wait_ge(s("gelu"), f + 1)
                    dve.wait_ge(s("conv"), f * 2 + 4)
                    nc.vector.tensor_tensor(cv[0][:, GAP:COLS], cv[0][:, GAP:COLS], cv[1][:, GAP:COLS], ALU.mult).then_inc(s("hid"), 1)
                    dve.wait_ge(s("hid_hi"), f + 1)
                    nc.vector.tensor_tensor(hid_lo[:, GAP:COLS], cv[0][:, GAP:COLS], hid_hi[:, GAP:COLS].bitcast(F32),
                                            ALU.subtract).then_inc(s("hid_lo"), 1)

                dve.sem_inc(s("conv"), 2)
                dve.sem_inc(s("hid"), 1)
                dve.sem_inc(s("hid_lo"), 1)
                dve.sem_inc(s("added"), 2)
                nc.vector.memset(acc[:], 0.0)
                nc.vector.memset(ss[:], 1.0).then_inc(s("acc_clear"), 1)
                dve.wait_ge(s("acc_clear"), 1)
                bodies(dve, step, lambda f, b: add_share(f))
                dve.wait_ge(s("squares"), TILES)
                ch = Chain(dve, s("dve_chain"))
                rsqrt_steps(nc, ch, ss[:], rstd[:], tmp[:], 1.0 / D)
                dve.wait_ge(s("x2_ready"), 16 * (TILES + 1))
                for m in range(TILES):
                    r = rows(m)
                    nc.vector.scalar_tensor_tensor(out=acc[0:r, m, :], in0=acc[0:r, m, :], scalar=rstd[0:r, m:m + 1],
                                                   in1=g_row[0:r, :], op0=ALU.mult, op1=ALU.mult).then_inc(s("scaled"), 1)


_INS = ["x_prompt", "x_sample", "cache_sb_k", "cache_sb_v", "state_ffn_conv", "g_pre_mix", "w_in", "ln_v_g", "ln_v_b",
        "w_s", "b_s", "w_gate", "b_gate", "w_branch_a", "w_branch_b", "w_o", "g_post_mix", "g_pre_ffn", "w_up",
        "w_conv", "b_conv", "w_down", "g_post_ffn"]
_OUTS = [("y_prompt", (1, SEQ, D)), ("y_sample", (1, DEC, D)),
         ("new_sb_k_prompt", (1, 1, SEQ, HEADS, DH)), ("new_sb_v_prompt", (1, 1, SEQ, HEADS, DH)),
         ("new_conv_prompt", (1, 1, 2, 2 * FF)),
         ("new_sb_k_sample", (1, 1, DEC, HEADS, DH)), ("new_sb_v_sample", (1, 1, DEC, HEADS, DH)),
         ("new_conv_sample", (1, 1, 2, 2 * FF)), ("new_gmlp_v_sample", (1, 1, DEC, D))]


def kernel(**inputs):
    import numpy as _np
    import concourse.bacc as _bacc
    from concourse import mybir as _mybir
    from concourse.bass_utils import run_bass_kernel_spmd as _run

    nc = _bacc.Bacc("TRN2", target_bir_lowering=False, num_devices=1)
    arrays, ins, outs = {}, {}, {}
    for name in _INS:
        v = _np.ascontiguousarray(inputs[name])
        arrays[f"in_{name}"] = v
        ins[name] = nc.dram_tensor(f"in_{name}", v.shape, _mybir.dt.from_np(v.dtype), kind="ExternalInput").ap()
    for name, shape in _OUTS:
        outs[name] = nc.dram_tensor(f"out_{name}", shape, _mybir.dt.float32, kind="ExternalOutput").ap()
    build_layer(nc, ins, outs)
    r = _run(nc, [arrays], core_ids=[0])
    return tuple(r.results[0][f"out_{name}"] for name, _ in _OUTS)
```

```python
from contextlib import ExitStack

import concourse.bass as bass
from concourse import mybir
from concourse.alu_op_type import AluOpType as ALU

ACT = mybir.ActivationFunctionType
F32 = mybir.dt.float32
F32R = mybir.dt.float32r
I32 = mybir.dt.int32

P = 128
D = 1024
KT = D // P
SEQ, DEC, PAST = 1024, 64, 2048
HEADS, DH = 16, 64
PAIRS = HEADS // 2
GROUPS = 8
FF = 2816
FT = FF // P
GAP = 2
COLS = GAP + SEQ + GAP + DEC
NCH = 3
CH = COLS // NCH
SCOL = GAP + SEQ + GAP
TILES = SEQ // P + 1
SLOT = 1024
FFN_SLOTS = 6
EPS = 1e-6
SCALE = DH ** -0.5
RSQRT_MAGIC = float(0x5F3759DF)


def rows(m):
    return P if m < TILES - 1 else DEC


def col(m):
    return GAP + m * P if m < TILES - 1 else SCOL


class Place:

    def __init__(self, nc, start, size):
        self.nc, self.at, self.end = nc, start, start + size

    def __call__(self, name, shape, dtype=F32):
        size = 4
        for n in shape[1:]:
            size *= n
        t = self.nc.alloc_sbuf_tensor_at(name, shape, dtype, offset=self.at)
        self.at += (size + 31) // 32 * 32
        assert self.at <= self.end, (name, self.at - self.end)
        return t


class Sems:

    def __init__(self, nc, stack, phase):
        self.nc, self.phase, self.known = nc, phase, {}
        stack.callback(self.give_back)

    def give_back(self):
        self.nc.clear_and_free_semaphores(list(self.known.values()))
        self.nc.all_engine_barrier()

    def __call__(self, name):
        if name not in self.known:
            self.known[name] = self.nc.alloc_semaphore(f"{self.phase}_{name}")
        return self.known[name]


class Chain:

    def __init__(self, eng, sem, start=0):
        self.eng, self.sem, self.n = eng, sem, start

    def step(self, ins):
        self.n += 1
        ins.then_inc(self.sem, 1)
        self.eng.wait_ge(self.sem, self.n)


class Weights:

    CREDIT = 4
    AHEAD = 2

    @staticmethod
    def buffers(phase, slots, raw_place, place):
        return (raw_place(f"{phase}_w_raw", [P, 2, SLOT]), place(f"{phase}_w_hi", [P, slots, SLOT], F32R),
                place(f"{phase}_w_lo", [P, slots, SLOT], F32R))

    def __init__(self, nc, s, buffers):
        self.nc = nc
        self.raw, self.hi, self.lo = buffers
        self.raw_ready = [s("raw_ready0"), s("raw_ready1")]
        self.split, self.passed = s("weights_split"), s("split_passed")

    def start_pool(self, pool, ahead=0):
        pool.sem_inc(self.split, self.CREDIT + 2 * ahead)

    def start_ahead(self, sp):
        for sem in self.raw_ready:
            sp.sem_inc(sem, 16)

    def load(self, sp, n, parity, src, tiles):
        sp.wait_ge(self.split, n * 2 + 2)
        sp.dma_start(self.raw[:, parity, :].rearrange("p (k c) -> p k c", k=tiles), src).then_inc(self.raw_ready[parity], 16)

    def split_one(self, pool, n, uses, slot, parity):
        pool.wait_ge(self.raw_ready[parity], (uses + 1) * 16)
        hold(pool, self.passed)
        self.nc.gpsimd.tensor_scalar(self.hi[:, slot, :], self.raw[:, parity, :], 1.0, 0.0,
                                     ALU.mult, ALU.add).then_inc(self.split, 1)
        pool.wait_ge(self.split, n * 2 + (self.CREDIT + 1))
        self.nc.gpsimd.tensor_tensor(self.lo[:, slot, :], self.raw[:, parity, :],
                                     self.hi[:, slot, :].bitcast(F32), ALU.subtract).then_inc(self.split, 1)

    def ready(self, pe, n):
        pe.wait_ge(self.split, n * 2 + (self.CREDIT + 2))


def hold(eng, passed):
    eng.sem_inc(passed)


def three_passes(nc, out, stat_hi, stat_lo, mov_hi, mov_lo, first, last):
    nc.tensor.matmul(out, stat_hi, mov_lo, start=first, stop=False)
    nc.tensor.matmul(out, stat_hi, mov_hi, start=False, stop=False)
    return nc.tensor.matmul(out, stat_lo, mov_hi, start=False, stop=last)


def rsqrt_steps(nc, chain, v, y, t, scale):
    vec = nc.vector
    chain.step(vec.tensor_scalar(v, v, scale, EPS, ALU.mult, ALU.add))
    chain.step(vec.tensor_scalar(t.bitcast(I32), v.bitcast(I32), 1, None, ALU.logical_shift_right))
    chain.step(vec.tensor_scalar(y.bitcast(I32), t.bitcast(I32), -1.0, RSQRT_MAGIC, ALU.mult, ALU.add))
    for _ in range(3):
        chain.step(vec.scalar_tensor_tensor(out=t, in0=y, scalar=-0.5, in1=y, op0=ALU.mult, op1=ALU.mult))
        chain.step(vec.tensor_tensor(t, t, v, ALU.mult))
        chain.step(vec.scalar_tensor_tensor(out=y, in0=t, scalar=1.5, in1=y, op0=ALU.add, op1=ALU.mult))


def clear_gaps(nc, eng, *arrays):
    for a in arrays:
        eng.memset(a[:, :, 0:GAP].bitcast(F32), 0.0)
        last = eng.memset(a[:, :, GAP + SEQ:SCOL].bitcast(F32), 0.0)
    return last


PAR = {"b_gate": 0, "b_s": 16, "b_conv": 24, "w_conv0": 128, "w_conv1": 172, "w_conv2": 256,
       "state0": 384, "state1": 428}


def build_layer(nc, a, o):
    base = (nc.sbuf_base + 63) // 64 * 64
    small = Place(nc, base, 3072)
    region = COLS * KT * 4 * 2
    r0 = base + 3072
    r1 = r0 + region
    rf = r1 + region
    f_size = nc.sbuf_usable_end - rf
    ident = small("ident", [P, P])
    par = small("par", [P, 512])

    def dram(name, shape):
        return nc.dram_tensor(name, shape, F32, kind="Internal").ap()

    u_dram = dram("u_scratch", (SEQ + DEC, D))
    q_dram = dram("q_scratch", (SEQ + DEC, D))
    ta_dram = dram("ta_scratch", (KT, P, COLS))
    gb_dram = dram("gb_scratch", (KT, P, COLS))
    x2_dram = dram("x2_scratch", (SEQ + DEC, D))

    def pair_of(name, start):
        pl = Place(nc, start, region)
        return pl(name + "_hi", [P, KT, COLS], F32R), pl(name + "_lo", [P, KT, COLS], F32R)

    hT = pair_of("hT", r0)
    yaT = pair_of("yaT", r1)
    ybT = pair_of("ybT", r0)
    mgT = pair_of("mergedT", r1)
    v_tok = nc.alloc_sbuf_tensor_at("v_tok", [P, TILES, D], F32, offset=rf)
    v_bytes = TILES * D * 4

    phase_project(nc, a, o, ident, par, hT, v_tok, u_dram, q_dram, r1, region, rf + v_bytes, f_size - v_bytes)
    phase_gating(nc, a, o, ident, par, v_tok, yaT, u_dram, rf + v_bytes, f_size - v_bytes)
    phase_gates(nc, a, par, hT, yaT, ta_dram, gb_dram, rf, f_size)
    phase_prompt_attention(nc, o, ident, ybT, q_dram, r1, region + f_size)
    phase_sample_attention(nc, a, o, ident, ybT, q_dram, r1, region + f_size)
    phase_merge(nc, a, ybT, mgT, ta_dram, gb_dram, rf, f_size)
    ffn_place = Place(nc, rf, f_size)
    ffn_ring = Weights.buffers("p8", FFN_SLOTS, ffn_place, ffn_place)
    phase_output(nc, a, ident, mgT, x2_dram, ffn_ring, r0, region, rf, f_size)
    phase_ffn(nc, a, o, ident, par, mgT, x2_dram, ffn_ring, ffn_place.at, r0, region, rf, f_size)


def phase_project(nc, a, o, ident, par, hT, v_tok, u_dram, q_dram, r1, r1_size, rf, rf_size):
    w_in = a["w_in"][0].rearrange("(k p) c -> p k c", p=P)
    with ExitStack() as ctx:
        s = Sems(nc, ctx, "p1")
        f = Place(nc, rf, rf_size)
        ring_place = Place(nc, r1, r1_size)
        ring = Weights(nc, s, Weights.buffers("p1", 8, f, ring_place))
        par_rows = ring_place("par_rows", [P, 4, P])
        g_row = f("g_pre_row", [P, D])
        lng = f("ln_g_row", [P, D])
        lnb = f("ln_b_row", [P, D])
        stage = f("stage", [P, 3, 512])
        ss = f("ss", [P, TILES])
        rstd = f("rstd", [P, TILES])
        tmp = f("rs_tmp", [P, TILES])
        stats = f("stats", [P, 2, 6])
        mv = f("mean_var", [P, TILES, 2])
        psA = ctx.enter_context(nc.psum_tensor("p1_psA", [P, 2, KT, P], F32))
        psB = ctx.enter_context(nc.psum_tensor("p1_psB", [P, 3, 512], F32))
        psP = ctx.enter_context(nc.psum_tensor("p1_psP", [P, 512], F32))
        x_tok = nc.alloc_sbuf_tensor_at("x_tok", [P, TILES, D], F32, offset=rf - TILES * D * 4)
        NM = 5
        NORM = 3
        with nc.Block() as block:

            @block.sync
            def _(sp):
                for m in range(TILES):
                    if m == NORM:
                        sp.dma_start(g_row[:, :], a["g_pre_mix"].to_broadcast([P, D])).then_inc(s("g_ready"), 16)
                    src = a["x_prompt"][0, m * P:(m + 1) * P, :] if m < TILES - 1 else a["x_sample"][0]
                    sp.dma_start(x_tok[0:rows(m), m, :], src).then_inc(s(f"x_ready{m}"), 16)
                with sp.Fori(0, NM) as i:
                    for n in range(8):
                        src = w_in[:, 2 * (n % 4):2 * (n % 4) + 2, bass.ds(i * D + (n // 4) * 512, 512)]
                        ring.load(sp, i * 8 + n, n % 2, src, 2)

            @block.gpsimd
            def _(pool):
                ring.start_pool(pool)
                nc.gpsimd.memset(ident[:], 0.0).then_inc(s("ident"), 1)
                pool.wait_ge(s("ident"), 1)
                nc.gpsimd.affine_select(out=ident[:], in_=ident[:], compare_op=ALU.not_equal, fill=1.0, base=0,
                                        pattern=[[-1, P]], channel_multiplier=1).then_inc(s("ident"), 1)
                with pool.Fori(0, NM) as i:
                    for n in range(8):
                        if n % 4 == 0:
                            pool.wait_ge(s("proj_ready"), i * 2 * TILES + (n // 4 + 1) * TILES)
                        ring.split_one(pool, i * 8 + n, i * 4 + n // 2, n, n % 2)

            @block.tensor
            def _(pe):
                pe.sem_inc(s("proj_ready"), 2 * TILES)
                pe.wait_ge(s("ident"), 2)
                for m in range(TILES):
                    pe.wait_ge(s("h_ready"), m + 1)
                    if m >= 2:
                        pe.wait_ge(s("hT_hi"), m - 1)
                        pe.wait_ge(s("hT_lo"), m - 1)
                    for k in range(KT):
                        last = nc.tensor.transpose(psA[:, m % 2, k, 0:rows(m)], x_tok[0:rows(m), m, k * P:(k + 1) * P],
                                                   ident[0:rows(m), 0:rows(m)])
                    last.then_inc(s("h_turned"), 1)
                pe.wait_ge(s("par_ready"), 16 * 8)
                for g in range(4):
                    last = nc.tensor.transpose(psP[:, g * P:(g + 1) * P], par_rows[:, g, :], ident[:, :])
                last.then_inc(s("par_turned"), 1)
                pe.wait_ge(s("hT_hi"), TILES)
                pe.wait_ge(s("hT_lo"), TILES)
                with pe.Fori(0, NM) as i:
                    for c in range(2):
                        ring.ready(pe, i * 8 + 4 * c + 3)
                        for m in range(TILES):
                            n = c * TILES + m
                            pe.wait_ge(s("proj_free"), i * 2 * TILES + n + 1)
                            for k in range(KT):
                                slot, at = 4 * c + k // 2, (k % 2) * 512
                                last = three_passes(
                                    nc, psB[0:rows(m), n % 3, :], hT[0][:, k, col(m):col(m) + rows(m)],
                                    hT[1][:, k, col(m):col(m) + rows(m)], ring.hi[:, slot, at:at + 512],
                                    ring.lo[:, slot, at:at + 512], k == 0, k == KT - 1)
                            last.then_inc(s("proj_ready"), 1)

            @block.scalar
            def _(act):
                act.sem_inc(s("proj_free"), 3)
                for b in range(3):
                    act.sem_inc(s(f"stage_free{b}"), 16)
                act.wait_ge(s("par_zero"), 1)
                for src, g, r, n in (("b_gate", 0, 0, 16), ("b_s", 0, 16, 8), ("b_conv", 0, 24, 44)):
                    v = a[src][0] if src == "b_s" else a[src][0].rearrange("(r c) -> r c", c=P)
                    act.dma_start(par_rows[r:r + n, g, :], v).then_inc(s("par_ready"), 16)
                for j, (g, r) in enumerate(((1, 0), (1, 44), (2, 0))):
                    act.dma_start(par_rows[r:r + 44, g, :], a["w_conv"][0, j].rearrange("(r c) -> r c", c=P)).then_inc(s("par_ready"), 16)
                for j in range(2):
                    act.dma_start(par_rows[44 * j:44 * j + 44, 3, :],
                                  a["state_ffn_conv"][0, 0, j].rearrange("(r c) -> r c", c=P)).then_inc(s("par_ready"), 16)
                act.dma_start(lng[:, :], a["ln_v_g"].to_broadcast([P, D])).then_inc(s("ln_ready"), 16)
                act.dma_start(lnb[:, :], a["ln_v_b"].to_broadcast([P, D])).then_inc(s("ln_ready"), 16)
                act.wait_ge(s("ss_zero"), 1)
                def hi(m):
                    act.wait_ge(s("h_turned"), m + 1)
                    nc.scalar.activation(hT[0][:, :, col(m):col(m) + rows(m)], psA[:, m % 2, :, 0:rows(m)],
                                         ACT.Copy).then_inc(s("hT_hi"), 1)

                for m in range(TILES):
                    act.wait_ge(s(f"x_ready{m}"), 16)
                    nc.scalar.activation(stage[:].rearrange("p n c -> p (n c)")[0:rows(m), 0:D], x_tok[0:rows(m), m, :],
                                         ACT.Square, accum_out=ss[0:rows(m), m:m + 1]).then_inc(s("squares"), 1)
                    act.wait_ge(s("squares"), m + 1)
                    if m > NORM:
                        hi(m - NORM - 1)
                for m in range(TILES - NORM - 1, TILES):
                    hi(m)

                def empty(first, func, where):
                    with act.Fori(0, 2) as c:
                        for m in range(TILES):
                            n = c * TILES + (first * 2 * TILES + m)
                            act.wait_ge(s("proj_ready"), n + (2 * TILES + 1))
                            if where is None:
                                nc.scalar.activation(v_tok[0:rows(m), m, bass.ds(c * 512, 512)], psB[0:rows(m), m % 3, :],
                                                     func).then_inc(s("proj_free"), 1)
                                continue
                            b = m % 3
                            use = (first - (first > 1)) * 6 + m // 3
                            act.wait_ge(s(f"stage_free{b}"), (c * 3 + (use + 1)) * 16)
                            nc.scalar.activation(stage[0:rows(m), b, :], psB[0:rows(m), m % 3, :],
                                                 func).then_inc(s("proj_free"), 1)
                            act.wait_ge(s("proj_free"), n + 4)
                            act.dma_start(where(m, c), stage[0:rows(m), b, :]).then_inc(s(f"stage_free{b}"), 16)

                def rows_of(dst):
                    return lambda m, c: dst[m * P:m * P + rows(m), bass.ds(c * 512, 512)]

                def out_rows(prompt, sample):
                    pr = prompt[0, 0].rearrange("t h d -> t (h d)")
                    sa = sample[0, 0].rearrange("t h d -> t (h d)")
                    return lambda m, c: (pr[m * P:(m + 1) * P, bass.ds(c * 512, 512)] if m < TILES - 1
                                         else sa[:, bass.ds(c * 512, 512)])

                empty(0, ACT.Gelu_apprx_tanh, rows_of(u_dram))
                empty(1, ACT.Gelu_apprx_tanh, None)
                empty(2, ACT.Copy, rows_of(q_dram))
                empty(3, ACT.Copy, out_rows(o["new_sb_k_prompt"], o["new_sb_k_sample"]))
                empty(4, ACT.Copy, out_rows(o["new_sb_v_prompt"], o["new_sb_v_sample"]))
                for b in range(3):
                    act.wait_ge(s(f"stage_free{b}"), 16 * (1 + 4 * 6))
                act.wait_ge(s("v_normed"), TILES)
                act.dma_start(o["new_gmlp_v_sample"][0, 0], v_tok[0:DEC, TILES - 1, :]).then_inc(s("gv_stored"), 16)
                act.wait_ge(s("gv_stored"), 16)

            @block.vector
            def _(dve):
                ch = Chain(dve, s("dve_chain"))
                nc.vector.memset(par_rows[:], 0.0).then_inc(s("par_zero"), 1)
                ch.step(nc.vector.memset(ss[:], 1.0))
                nc.vector.sem_inc(s("ss_zero"), 1)
                ch.step(clear_gaps(nc, nc.vector, *hT))

                def lo(m):
                    c = slice(col(m), col(m) + rows(m))
                    dve.wait_ge(s("hT_hi"), m + 1)
                    nc.vector.tensor_tensor(hT[1][:, :, c], psA[:, m % 2, :, 0:rows(m)], hT[0][:, :, c].bitcast(F32),
                                            ALU.subtract).then_inc(s("hT_lo"), 1)

                for m in range(TILES):
                    r = rows(m)
                    if m % NORM == 0:
                        g = slice(m, m + NORM)
                        dve.wait_ge(s("squares"), m + NORM)
                        rsqrt_steps(nc, ch, ss[:, g], rstd[:, g], tmp[:, g], 1.0 / D)
                    if m == 0:
                        dve.wait_ge(s("g_ready"), 16)
                    nc.vector.scalar_tensor_tensor(out=x_tok[0:r, m, :], in0=x_tok[0:r, m, :], scalar=rstd[0:r, m:m + 1],
                                                   in1=g_row[0:r, :], op0=ALU.mult, op1=ALU.mult).then_inc(s("h_ready"), 1)
                    if m >= 2:
                        lo(m - 2)
                lo(TILES - 2)
                lo(TILES - 1)
                dve.wait_ge(s("par_turned"), 1)
                nc.vector.tensor_copy(par[:], psP[:]).then_inc(s("par_copied"), 1)
                dve.wait_ge(s("ln_ready"), 32)
                ch.step(nc.vector.memset(mv[:], 1.0))
                for m in range(TILES):
                    r = rows(m)
                    dve.wait_ge(s("proj_free"), 3 + 2 * TILES + TILES + m + 1)
                    for h in range(2):
                        ch.step(nc.vector.bn_stats(stats[0:r, h, :], v_tok[0:r, m, h * 512:(h + 1) * 512]))
                    ch.step(nc.vector.bn_aggr(mv[0:r, m, :], stats[0:r, :, :].rearrange("p a b -> p (a b)")))
                ch.step(nc.vector.tensor_copy(ss[:], mv[:, :, 1]))
                rsqrt_steps(nc, ch, ss[:], rstd[:], tmp[:], 1.0)
                for m in range(TILES):
                    r = rows(m)
                    ch.step(nc.vector.scalar_tensor_tensor(out=v_tok[0:r, m, :], in0=v_tok[0:r, m, :], scalar=mv[0:r, m, 0:1],
                                                           in1=lng[0:r, :], op0=ALU.subtract, op1=ALU.mult))
                    nc.vector.scalar_tensor_tensor(out=v_tok[0:r, m, :], in0=v_tok[0:r, m, :], scalar=rstd[0:r, m:m + 1],
                                                   in1=lnb[0:r, :], op0=ALU.mult, op1=ALU.add).then_inc(s("v_normed"), 1)


def phase_gating(nc, a, o, ident, par, v_tok, yaT, u_dram, rf, rf_size):
    YA = 3
    LAG = 2
    with ExitStack() as ctx:
        s = Sems(nc, ctx, "p2")
        f = Place(nc, rf, rf_size)
        ws = f("w_s_rows", [P, GROUPS, P])
        wsT = f("w_s_turned", [P, GROUPS, P])
        u = f("u_tok", [P, 2, D])
        ya = f("ya_tok", [P, YA, D])
        psM = ctx.enter_context(nc.psum_tensor("p2_psM", [P, 2, D], F32))
        psT = ctx.enter_context(nc.psum_tensor("p2_psT", [P, 2, KT, P], F32))
        with nc.Block() as block:

            @block.sync
            def _(sp):
                sp.dma_start(ws[:], a["w_s"][0].rearrange("g t s -> t g s")).then_inc(s("ws_ready"), 16)
                for m in range(TILES):
                    if m >= 2:
                        sp.wait_ge(s("ya_ready"), m - 1)
                    sp.dma_start(u[0:rows(m), m % 2, :], u_dram[m * P:m * P + rows(m), :]).then_inc(s(f"u_ready{m % 2}"), 16)

            @block.gpsimd
            def _(pool):
                pool.wait_ge(s("ws_ready"), 16)
                nc.gpsimd.affine_select(out=ws[:], in_=ws[:], compare_op=ALU.is_ge, fill=0.0, base=0,
                                        pattern=[[0, GROUPS], [-1, P]], channel_multiplier=1).then_inc(s("ws_masked"), 1)
                for m in range(TILES):
                    r = rows(m)
                    pool.wait_ge(s("biased"), m + 1)
                    pool.wait_ge(s(f"u_ready{m % 2}"), 16 * (m // 2 + 1))
                    nc.gpsimd.tensor_tensor(ya[0:r, m % YA, :], ya[0:r, m % YA, :], u[0:r, m % 2, :],
                                            ALU.mult).then_inc(s("ya_ready"), 1)

            @block.tensor
            def _(pe):
                pe.wait_ge(s("ws_masked"), 1)
                for g in range(GROUPS):
                    last = nc.tensor.transpose(psT[:, 0, g, :], ws[:, g, :], ident[:, :])
                last.then_inc(s("ws_turned"), 1)
                pe.wait_ge(s("wsT_ready"), 1)

                def mix(m):
                    r = rows(m)
                    if m >= 2:
                        pe.wait_ge(s("biased"), m - 1)
                    for g in range(GROUPS):
                        last = nc.tensor.matmul(psM[0:r, m % 2, g * P:(g + 1) * P], wsT[0:r, g, 0:r],
                                                v_tok[0:r, m, g * P:(g + 1) * P], start=True, stop=True)
                    last.then_inc(s("mixed"), 1)

                mix(0)
                mix(1)
                for m in range(TILES):
                    if m + 2 < TILES:
                        mix(m + 2)
                    pe.wait_ge(s("ya_ready"), m + 1)
                    if m >= 2:
                        pe.wait_ge(s("yaT_lo"), m - 1)
                    for k in range(KT):
                        last = nc.tensor.transpose(psT[:, m % 2, k, 0:rows(m)], ya[0:rows(m), m % YA, k * P:(k + 1) * P],
                                                   ident[0:rows(m), 0:rows(m)])
                    last.then_inc(s("ya_turned"), 1)

            @block.scalar
            def _(act):
                act.wait_ge(s("ws_turned"), 1)
                nc.scalar.activation(wsT[:], psT[:, 0], ACT.Copy).then_inc(s("wsT_ready"), 1)
                for m in range(TILES):
                    act.wait_ge(s("ya_turned"), m + 1)
                    nc.scalar.activation(yaT[0][:, :, col(m):col(m) + rows(m)], psT[:, m % 2, :, 0:rows(m)],
                                         ACT.Copy).then_inc(s("yaT_hi"), 1)

            @block.vector
            def _(dve):
                clear_gaps(nc, nc.vector, *yaT).then_inc(s("gaps"), 1)

                def lo(m):
                    c = slice(col(m), col(m) + rows(m))
                    dve.wait_ge(s("yaT_hi"), m + 1)
                    nc.vector.tensor_tensor(yaT[1][:, :, c], psT[:, m % 2, :, 0:rows(m)], yaT[0][:, :, c].bitcast(F32),
                                            ALU.subtract).then_inc(s("yaT_lo"), 1)

                for m in range(TILES):
                    r = rows(m)
                    dve.wait_ge(s("mixed"), m + 1)
                    if m >= YA:
                        dve.wait_ge(s("ya_turned"), m - YA + 1)
                    bias = par[0:r, PAR["b_s"]:PAR["b_s"] + GROUPS].unsqueeze(2).to_broadcast([r, GROUPS, P])
                    nc.vector.tensor_tensor(ya[0:r, m % YA, :].rearrange("p (g c) -> p g c", g=GROUPS),
                                            psM[0:r, m % 2, :].rearrange("p (g c) -> p g c", g=GROUPS), bias,
                                            ALU.add).then_inc(s("biased"), 1)
                    if m >= LAG:
                        lo(m - LAG)
                for m in range(TILES - LAG, TILES):
                    lo(m)


def feature_product(nc, pe, out, ring, slot, act_pair):
    for ch in range(NCH):
        c = slice(ch * CH, (ch + 1) * CH)
        for k in range(KT):
            w = slice(k * P, (k + 1) * P)
            last = three_passes(nc, out[:, ch, 0:CH], ring.hi[:, slot, w], ring.lo[:, slot, w],
                                act_pair[0][:, k, c], act_pair[1][:, k, c], k == 0, k == KT - 1)
    return last


def by_chunks(t):
    return t.rearrange("p (n c) -> p n c", n=NCH)


def phase_gates(nc, a, par, hT, yaT, ta_dram, gb_dram, rf, rf_size):
    w_gate = a["w_gate"][0].rearrange("(k p) c -> p k c", p=P)
    w_a = a["w_branch_a"][0].rearrange("(k p) c -> p k c", p=P)
    with ExitStack() as ctx:
        s = Sems(nc, ctx, "p3")
        f = Place(nc, rf, rf_size)
        ring = Weights(nc, s, Weights.buffers("p3", 6, f, f))
        ga = f("g_a", [P, COLS])
        gb = f("g_b", [P, COLS])
        ps = ctx.enter_context(nc.psum_tensor("p3_ps", [P, 2, 4, 512], F32))
        with nc.Block() as block:

            @block.sync
            def _(sp):
                with sp.Fori(0, KT // 2) as i:
                    for n in range(6):
                        kind, j = n % 3, i * 2 * P + (n // 3) * P
                        src = w_a[:, :, bass.ds(j, P)] if kind == 2 else w_gate[:, :, bass.ds(j + kind * D, P)]
                        ring.load(sp, i * 6 + n, n % 2, src, KT)

            @block.gpsimd
            def _(pool):
                ring.start_pool(pool)
                with pool.Fori(0, KT // 2) as i:
                    for n in range(6):
                        pool.wait_ge(s("product"), i * 6 + (n + 1))
                        ring.split_one(pool, i * 6 + n, i * 3 + n // 2, n, n % 2)

            @block.tensor
            def _(pe):
                pe.sem_inc(s("product"), 6)
                with pe.Fori(0, KT // 2) as i:
                    for n in range(6):
                        ring.ready(pe, i * 6 + n)
                        pe.wait_ge(s("ps_free"), i * 6 + n + 1)
                        last = feature_product(nc, pe, ps[:, n % 2], ring, n, yaT if n % 3 == 2 else hT)
                        last.then_inc(s("product"), 1)

            @block.scalar
            def _(act):
                act.sem_inc(s("ta_stored"), 16)
                act.sem_inc(s("gb_stored"), 16)
                with act.Fori(0, KT // 2) as i:
                    for u in range(2):
                        act.wait_ge(s("product"), i * 6 + (3 * u + 7))
                        act.wait_ge(s("ta_stored"), (i * 2 + (u + 1)) * 16)
                        nc.scalar.activation(by_chunks(ga[:, :]), ps[:, (3 * u) % 2, 0:NCH, 0:CH], ACT.Sigmoid,
                                             bias=par[:, bass.ds(i * 2 + (PAR["b_gate"] + u), 1)]).then_inc(s("gate"), 1)
                        act.wait_ge(s("product"), i * 6 + (3 * u + 8))
                        act.wait_ge(s("gb_stored"), (i * 2 + (u + 1)) * 16)
                        nc.scalar.activation(by_chunks(gb[:, :]), ps[:, (3 * u + 1) % 2, 0:NCH, 0:CH], ACT.Sigmoid,
                                             bias=par[:, bass.ds(i * 2 + (PAR["b_gate"] + KT + u), 1)]).then_inc(s("gate"), 1)
                        act.wait_ge(s("gate"), i * 4 + (2 * u + 2))
                        act.dma_start(gb_dram[bass.ds(i * 2 + u, 1), :, :].rearrange("o p c -> (o p) c"), gb[:, :]).then_inc(s("gb_stored"), 16)
                        act.wait_ge(s("ta_ready"), i * 2 + (u + 1))
                        act.dma_start(ta_dram[bass.ds(i * 2 + u, 1), :, :].rearrange("o p c -> (o p) c"), ga[:, :]).then_inc(s("ta_stored"), 16)
                act.wait_ge(s("ta_stored"), 16 * (KT + 1))
                act.wait_ge(s("gb_stored"), 16 * (KT + 1))

            @block.vector
            def _(dve):
                dve.sem_inc(s("ps_free"), 2)
                with dve.Fori(0, KT // 2) as i:
                    for u in range(2):
                        dve.wait_ge(s("gate"), i * 4 + (2 * u + 1))
                        nc.vector.sem_inc(s("ps_free"), 1)
                        dve.wait_ge(s("gate"), i * 4 + (2 * u + 2))
                        nc.vector.sem_inc(s("ps_free"), 1)
                        dve.wait_ge(s("product"), i * 6 + (3 * u + 9))
                        nc.vector.tensor_tensor(by_chunks(ga[:, :]), ps[:, (3 * u + 2) % 2, 0:NCH, 0:CH],
                                                by_chunks(ga[:, :]), ALU.mult).then_inc(s("ta_ready"), 1)
                        dve.wait_ge(s("ta_ready"), i * 2 + (u + 1))
                        nc.vector.sem_inc(s("ps_free"), 1)


def phase_prompt_attention(nc, o, ident, ybT, q_dram, start, size):
    QT = SEQ // P
    STEPS = 2 * QT
    SCAN_LAG, WEIGH_LAG, TURN_LAG, AV_LAG = 1, 2, 3, 4
    ORDER = (1, 0, 2, 3, 5, 7, 6, 4)
    k_rows = o["new_sb_k_prompt"][0, 0].rearrange("(n p) h d -> p n (h d)", p=P)
    v_rows = o["new_sb_v_prompt"][0, 0].rearrange("(n p) h d -> p n (h d)", p=P)
    q_rows = q_dram[0:SEQ, :].rearrange("(n p) c -> p n c", p=P)
    with ExitStack() as ctx:
        s = Sems(nc, ctx, "p4")
        f = Place(nc, start, size)
        raw_k = f("p4_raw_k", [P, QT, P])
        raw_q = f("p4_raw_q", [P, QT, P])
        raw_v = f("p4_raw_v", [P, QT, P])
        twice = f("p4_twice", [P, 2, QT, 2, DH])
        kT_hi = f("p4_kT_hi", [P, 2, SEQ], F32R)
        kT_lo = f("p4_kT_lo", [P, 2, SEQ], F32R)
        qT = f("p4_qT", [P, 2, SEQ], F32R)
        v2 = f("p4_v", [P, 2, QT, 2, DH], F32R)
        nb = f("p4_one_minus_beta", [P, 4, SEQ])
        rest = f("p4_rest", [P, 2, SEQ])
        wt = f("p4_weights", [P, 8, SEQ])
        aT = f("p4_aT", [P, 2, QT, 2, P], F32R)
        ytmp = f("p4_ytmp", [64, 2, 256])
        ysum = f("p4_ysum", [64, 2, 256])
        yb = f("p4_yb", [P, SEQ])
        psZ = ctx.enter_context(nc.psum_tensor("p4_psZ", [P, 2, SEQ], F32))
        psT = ctx.enter_context(nc.psum_tensor("p4_psT", [P, 2, 4, P], F32))
        psY = ctx.enter_context(nc.psum_tensor("p4_psY", [P, 512], F32))
        psP = ctx.enter_context(nc.psum_tensor("p4_psP", [P, 4, P], F32))

        def groups_before(u):
            return sum(1 if ORDER[x % QT] < 4 else 2 for x in range(u))

        NG = groups_before(STEPS)

        def lagged(u, lag):
            return (u - lag) % STEPS, (u - lag) < 0

        def bodies(eng, body, tail):
            body(0, True, False)
            with eng.Fori(1, PAIRS - 1) as p:
                body(p, False, False)
            body(PAIRS - 1, False, True)
            tail()

        def prep_piece(u):
            if 3 <= u < 7:
                return u - 3, 1
            if 11 <= u < 15:
                return u - 11, 0
            return None

        with nc.Block() as block:

            @block.sync
            def _(sp):
                def load(p, after):
                    c = bass.ds(p * P, P)
                    if after is not None:
                        sp.wait_ge(s("doubled"), after * 4 + 4)
                        sp.wait_ge(s("v_split"), after * 4 + 4)
                    sp.dma_start(raw_k[:], k_rows[:, :, c]).then_inc(s("raw_k"), 16)
                    sp.dma_start(raw_q[:], q_rows[:, :, c]).then_inc(s("raw_q"), 16)
                    sp.dma_start(raw_v[:], v_rows[:, :, c]).then_inc(s("raw_v"), 16)

                load(0, None)
                with sp.Fori(1, PAIRS) as p:
                    load(p, p - 1)

            @block.tensor
            def _(pe):
                def turn_piece(h, piece, parity):
                    which, g = piece // 2, piece % 2
                    pe.wait_ge(s("doubled"), h * 2 + (which + 1))
                    pe.wait_ge(s("prep_lo"), h * 4 + (piece + 1))
                    for t in range(4):
                        last = nc.tensor.transpose(psP[:, t, :], twice[:, which, 4 * g + t].rearrange("p a d -> p (a d)"),
                                                   ident[:, :])
                    last.then_inc(s("prep_turned"), 1)

                def z(p, u):
                    i, par = ORDER[u % QT], u // QT
                    h = p * 2 + par
                    pe.wait_ge(s("prep_lo"), h * 4 + 5)
                    pe.wait_ge(s("beta"), p * STEPS + (u + 1))
                    keys = (i + 1) * P
                    for c in range(0, keys, 512):
                        n = max(min(512, keys - c), 256)
                        stat = qT[:, par, i * P:(i + 1) * P]
                        nc.tensor.matmul(psZ[:, u % 2, c:c + n], stat, kT_lo[:, par, c:c + n], start=True, stop=False)
                        last = nc.tensor.matmul(psZ[:, u % 2, c:c + n], stat, kT_hi[:, par, c:c + n], start=False, stop=True)
                    last.then_inc(s("z"), 1)

                def turn(p, u):
                    i = ORDER[u % QT]
                    pe.wait_ge(s("weights"), p * STEPS + (u + 3))
                    g0 = groups_before(u)
                    for g in range((i + 4) // 4):
                        pe.wait_ge(s("aT_lo"), p * NG + (g0 + g + 1))
                        for t in range(4 * g, min(4 * g + 4, i + 1)):
                            last = nc.tensor.transpose(psT[:, (g0 + g) % 2, t % 4, :], wt[:, u % 8, t * P:(t + 1) * P],
                                                       ident[:, :])
                        last.then_inc(s("turned"), 1)

                def av(p, u):
                    i, par = ORDER[u % QT], u // QT
                    g1 = groups_before(u + 1)
                    pe.wait_ge(s("aT_lo"), p * NG + (g1 + 2))
                    pe.wait_ge(s("v_split"), p * 4 + (2 * par + 2))
                    pe.wait_ge(s("y_first"), p * STEPS + (u + 1))
                    for t in range(i + 1):
                        last = nc.tensor.matmul(psY[:, 0:256], v2[:, par, t].rearrange("p a d -> p (a d)"),
                                                aT[:, u % 2, t].rearrange("p a q -> p (a q)"), start=(t == 0), stop=(t == i))
                    last.then_inc(s("av"), 1)

                def body(p, first, last):
                    for u in range(STEPS):
                        z(p, u)
                        v, old = lagged(u, TURN_LAG)
                        if not (old and first):
                            turn(p - 1 if old else p, v)
                        piece = prep_piece(u)
                        if piece and not (last and piece[1] == 0):
                            turn_piece(p * 2 + (1 if piece[1] else 2), *piece)
                        v, old = lagged(u, AV_LAG)
                        if not (old and first):
                            av(p - 1 if old else p, v)

                def tail():
                    for u in range(STEPS - AV_LAG, STEPS):
                        if u + AV_LAG - TURN_LAG < STEPS:
                            turn(PAIRS - 1, u + AV_LAG - TURN_LAG)
                        av(PAIRS - 1, u)

                pe.sem_inc(s("av"), 2)
                for piece in range(4):
                    turn_piece(0, piece, 0)
                bodies(pe, body, tail)

            @block.scalar
            def _(act):
                def prep_hi(h, piece, par):
                    which, g = piece // 2, piece % 2
                    act.wait_ge(s("prep_turned"), h * 4 + (piece + 1))
                    dst = (qT if which else kT_hi)[:, par, 512 * g:512 * g + 512]
                    nc.scalar.activation(dst, psP[:].rearrange("p t c -> p (t c)"), ACT.Copy).then_inc(s("prep_hi"), 1)

                def sigmoids(p, u):
                    n = (ORDER[u % QT] + 1) * P
                    act.wait_ge(s("z"), p * STEPS + (u + 1))
                    act.wait_ge(s("scanned"), p * STEPS + (u + 1))
                    nc.scalar.activation(nb[:, u % 4, 0:n], psZ[:, u % 2, 0:n], ACT.Sigmoid, scale=-SCALE).then_inc(s("nb"), 1)
                    nc.scalar.activation(wt[:, u % 8, 0:n], psZ[:, u % 2, 0:n], ACT.Sigmoid, scale=SCALE).then_inc(s("beta"), 1)

                def split_hi(p, u):
                    i = ORDER[u % QT]
                    g0 = groups_before(u)
                    act.wait_ge(s("av"), p * STEPS + (u + 1))
                    for g in range((i + 4) // 4):
                        n = min(4, i + 1 - 4 * g)
                        act.wait_ge(s("turned"), p * NG + (g0 + g + 1))
                        nc.scalar.activation(aT[:, u % 2, 4 * g:4 * g + n, 0, :], psT[:, (g0 + g) % 2, 0:n, :],
                                             ACT.Copy).then_inc(s("aT_hi"), 1)

                def y_low_rows(p, u):
                    act.wait_ge(s("av"), p * STEPS + (u + 3))
                    nc.scalar.activation(ytmp[:, u % 2, :], psY[64:128, 0:256], ACT.Copy).then_inc(s("y_low"), 1)

                def y_hi(p):
                    act.wait_ge(s("y"), (p + 1) * STEPS)
                    nc.scalar.activation(ybT[0][:, bass.ds(p, 1), GAP:GAP + SEQ].rearrange("p o c -> p (o c)"), yb[:, :],
                                         ACT.Copy).then_inc(s("yb_hi"), 1)

                def body(p, first, last):
                    for u in range(STEPS):
                        sigmoids(p, u)
                        v, old = lagged(u, TURN_LAG)
                        if not (old and first):
                            split_hi(p - 1 if old else p, v)
                        piece = prep_piece(u)
                        if piece and not (last and piece[1] == 0):
                            prep_hi(p * 2 + (1 if piece[1] else 2), *piece)
                        v, old = lagged(u, AV_LAG)
                        if not (old and first):
                            y_low_rows(p - 1 if old else p, v)
                            if v == STEPS - 1:
                                y_hi(p - 1)

                def tail():
                    q = PAIRS - 1
                    for u in range(STEPS - AV_LAG, STEPS):
                        if u + AV_LAG - TURN_LAG < STEPS:
                            split_hi(q, u + AV_LAG - TURN_LAG)
                        y_low_rows(q, u)
                    y_hi(q)

                act.sem_inc(s("beta"), 2)
                for piece in range(4):
                    prep_hi(0, piece, 0)
                bodies(act, body, tail)

            @block.gpsimd
            def _(pool):
                def split_v_hi(p, par, after):
                    pool.wait_ge(s("raw_v"), p * 16 + 16)
                    if after is not None:
                        pool.wait_ge(s("av"), after + 2)
                        hold(pool, s("pool_passed"))
                    nc.gpsimd.tensor_scalar(v2[:, par, :, 0, :], raw_v[:, :, par * DH:(par + 1) * DH], 1.0, 0.0,
                                            ALU.mult, ALU.add).then_inc(s("v_split"), 1)

                def split_v_lo(h, par):
                    pool.wait_ge(s("v_split"), h * 2 + 1)
                    nc.gpsimd.tensor_tensor(v2[:, par, :, 1, :], raw_v[:, :, par * DH:(par + 1) * DH], v2[:, par, :, 0, :].bitcast(F32),
                                            ALU.subtract).then_inc(s("v_split"), 1)

                def masks(p, u):
                    d = slice(ORDER[u % QT] * P, (ORDER[u % QT] + 1) * P)
                    pool.wait_ge(s("nb"), p * STEPS + (u + 1))
                    hold(pool, s("pool_passed"))
                    nc.gpsimd.affine_select(out=nb[:, u % 4, d], in_=nb[:, u % 4, d], compare_op=ALU.is_gt, fill=1.0,
                                            base=0, pattern=[[-1, P]], channel_multiplier=1).then_inc(s("nb_masked"), 1)
                    pool.wait_ge(s("beta"), p * STEPS + (u + 3))
                    hold(pool, s("pool_passed"))
                    nc.gpsimd.affine_select(out=wt[:, u % 8, d], in_=wt[:, u % 8, d], compare_op=ALU.is_gt, fill=0.0,
                                            base=0, pattern=[[-1, P]], channel_multiplier=1).then_inc(s("beta_masked"), 1)

                def weigh(p, u):
                    n = (ORDER[u % QT] + 1) * P
                    pool.wait_ge(s("scanned"), p * STEPS + (u + 5))
                    pool.wait_ge(s("beta_masked"), p * STEPS + (u + 1))
                    nc.gpsimd.tensor_tensor(wt[:, u % 8, 0:n - 1], wt[:, u % 8, 0:n - 1], rest[:, u % 2, 1:n],
                                            ALU.mult).then_inc(s("weights"), 1)

                def body(p, first, last):
                    for u in range(STEPS):
                        v, old = lagged(u, WEIGH_LAG)
                        if not (old and first):
                            weigh(p - 1 if old else p, v)
                        masks(p, u)
                        if u == AV_LAG + 1:
                            split_v_hi(p, 1, p * STEPS)
                        if u == AV_LAG + 2:
                            split_v_lo(p * 2 + 1, 1)
                        if u == QT + AV_LAG + 1 and not last:
                            split_v_hi(p + 1, 0, p * STEPS + QT)
                        if u == QT + AV_LAG + 2 and not last:
                            split_v_lo(p * 2 + 2, 0)

                def tail():
                    for u in range(STEPS - WEIGH_LAG, STEPS):
                        weigh(PAIRS - 1, u)

                pool.sem_inc(s("weights"), 2)
                split_v_hi(0, 0, None)
                split_v_lo(0, 0)
                bodies(pool, body, tail)

            @block.vector
            def _(dve):
                def double(h, p, which, par, first=False):
                    dve.wait_ge(s("raw_q" if which else "raw_k"), p * 16 + 16)
                    if not first:
                        dve.wait_ge(s("prep_turned"), h * 4 - 4 + (2 * which + 2))
                    src = (raw_q if which else raw_k)[:, :, par * DH:(par + 1) * DH]
                    nc.vector.tensor_copy(twice[:, which], src.unsqueeze(2).to_broadcast([P, QT, 2, DH])).then_inc(s("doubled"), 1)

                def prep_lo(h, piece, par):
                    which, g = piece // 2, piece % 2
                    dve.wait_ge(s("prep_hi"), h * 4 + (piece + 1))
                    c = slice(512 * g, 512 * g + 512)
                    flat = psP[:].rearrange("p t c -> p (t c)")
                    if which:
                        nc.vector.tensor_tensor(qT[64:128, par, c], flat[64:128, :], qT[64:128, par, c].bitcast(F32),
                                                ALU.subtract).then_inc(s("prep_lo"), 1)
                    else:
                        nc.vector.tensor_tensor(kT_lo[:, par, c], flat, kT_hi[:, par, c].bitcast(F32),
                                                ALU.subtract).then_inc(s("prep_lo"), 1)

                def scan(p, u):
                    n = (ORDER[u % QT] + 1) * P
                    dve.wait_ge(s("nb_masked"), p * STEPS + (u + 1))
                    dve.wait_ge(s("weights"), p * STEPS + (u + 1))
                    src = nb[:, u % 4, n - 1::-1]
                    nc.vector.tensor_tensor_scan(rest[:, u % 2, n - 1::-1], src, src, 1.0, ALU.mult,
                                                 ALU.bypass).then_inc(s("scanned"), 1)

                def split_lo(p, u):
                    i, g0 = ORDER[u % QT], groups_before(u)
                    for g in range((i + 4) // 4):
                        n = min(4, i + 1 - 4 * g)
                        dve.wait_ge(s("aT_hi"), p * NG + (g0 + g + 1))
                        t = slice(4 * g, 4 * g + n)
                        nc.vector.tensor_tensor(aT[:, u % 2, t, 1, :], psT[:, (g0 + g) % 2, 0:n, :],
                                                aT[:, u % 2, t, 0, :].bitcast(F32), ALU.subtract).then_inc(s("aT_lo"), 1)

                def y_sum(p, u, wait_yb):
                    i, par = ORDER[u % QT], u // QT
                    dve.wait_ge(s("y_low"), p * STEPS + (u + 1))
                    nc.vector.tensor_tensor(ysum[:, u % 2, :], psY[0:64, 0:256], ytmp[:, u % 2, :], ALU.add).then_inc(s("y_first"), 1)
                    dve.wait_ge(s("y_first"), p * STEPS + (u + 2))
                    if wait_yb:
                        dve.wait_ge(s("yb_hi"), p)
                        dve.wait_ge(s("yb_lo"), p)
                    nc.vector.tensor_tensor(yb[64 * par:64 * par + 64, i * P:(i + 1) * P], ysum[:, u % 2, 0:P],
                                            ysum[:, u % 2, P:2 * P], ALU.add).then_inc(s("y"), 1)

                def y_lo(p):
                    dve.wait_ge(s("yb_hi"), p + 1)
                    pair = bass.ds(p, 1)
                    nc.vector.tensor_tensor(ybT[1][:, pair, GAP:GAP + SEQ].rearrange("p o c -> p (o c)"), yb[:, :],
                                            ybT[0][:, pair, GAP:GAP + SEQ].rearrange("p o c -> p (o c)").bitcast(F32),
                                            ALU.subtract).then_inc(s("yb_lo"), 1)

                def body(p, first, last):
                    for u in range(STEPS):
                        v, old = lagged(u, SCAN_LAG)
                        if not (old and first):
                            scan(p - 1 if old else p, v)
                        v, old = lagged(u, TURN_LAG)
                        if not (old and first):
                            split_lo(p - 1 if old else p, v)
                        if u in (1, 2):
                            double(p * 2 + 1, p, u - 1, 1)
                        if u in (9, 10) and not last:
                            double(p * 2 + 2, p + 1, u - 9, 0)
                        piece = prep_piece(u)
                        if piece and not (last and piece[1] == 0):
                            prep_lo(p * 2 + (1 if piece[1] else 2), *piece)
                        v, old = lagged(u, AV_LAG)
                        if not (old and first):
                            y_sum(p - 1 if old else p, v, v == 0 and not first)
                            if v == STEPS - 1:
                                y_lo(p - 1)

                def tail():
                    q = PAIRS - 1
                    for u in range(STEPS - SCAN_LAG, STEPS):
                        scan(q, u)
                    for u in range(STEPS - AV_LAG, STEPS):
                        if u + AV_LAG - TURN_LAG < STEPS:
                            split_lo(q, u + AV_LAG - TURN_LAG)
                        y_sum(q, u, False)
                    y_lo(q)

                dve.sem_inc(s("prep_lo"), 1)
                dve.sem_inc(s("scanned"), 4)
                dve.sem_inc(s("aT_lo"), 2)
                dve.sem_inc(s("y_first"), 1)
                clear_gaps(nc, nc.vector, *ybT).then_inc(s("gaps"), 1)
                double(0, 0, 0, 0, True)
                double(0, 0, 1, 0, True)
                for piece in range(4):
                    prep_lo(0, piece, 0)
                bodies(dve, body, tail)


def phase_sample_attention(nc, a, o, ident, ybT, q_dram, start, size):
    KEYS = PAST + DEC
    TK = PAST // P + 1
    GR = [(0, 4), (4, 8), (8, 12), (12, 16), (16, 17)]
    G = len(GR)
    ITEMS = [("A", 0), ("A", 1), ("K", 0), ("A", 2), ("K", 1), ("A", 3), ("K", 2), ("A", 4), ("K", 3), ("K", 4)]
    BANKS = 3
    HALF = 1024
    ZG = [(0, 1024, (512, 512)), (1024, 800, (512, 288)), (1824, 288, (288,))]
    caches = [(a["cache_sb_k"][0, 0].rearrange("(n p) h d -> p n (h d)", p=P),
               o["new_sb_k_sample"][0, 0].rearrange("t h d -> t (h d)")),
              (a["cache_sb_v"][0, 0].rearrange("(n p) h d -> p n (h d)", p=P),
               o["new_sb_v_sample"][0, 0].rearrange("t h d -> t (h d)"))]
    with ExitStack() as ctx:
        s = Sems(nc, ctx, "p5")
        f = Place(nc, start, size)
        raw_k = f("p5_raw_k", [P, 2, TK, P])
        raw_v = f("p5_raw_v", [P, TK, P])
        raw_q = f("p5_raw_q", [64, 2, P])
        q_hi = f("p5_q_hi", [P, P], F32R)
        q_lo = f("p5_q_lo", [P, P], F32R)
        kT_hi = f("p5_kT_hi", [P, KEYS], F32R)
        kT_lo = f("p5_kT_lo", [P, KEYS], F32R)
        v2 = f("p5_v", [P, 2, TK, 2, P], F32R)
        nb = f("p5_one_minus_beta", [P, KEYS])
        rest = f("p5_rest", [P, KEYS])
        wt = f("p5_weights", [P, 2, KEYS])
        aT = f("p5_aT", [P, TK, 2, P], F32R)
        seen = f("p5_seen", [P, 2, DEC])
        ytmp = f("p5_ytmp", [P, P])
        yb = f("p5_yb", [P, DEC])
        psZ = ctx.enter_context(nc.psum_tensor("p5_psZ", [P, 2, 1024], F32))
        psR = ctx.enter_context(nc.psum_tensor("p5_psR", [P, BANKS, 4, P], F32))
        psY = ctx.enter_context(nc.psum_tensor("p5_psY", [P, 512], F32))
        QCOL = P

        def bodies(eng, step):
            step(-1, 1)
            step(0, 0)
            with eng.Fori(0, 3) as i:
                step(i * 2 + 1, 1)
                step(i * 2 + 2, 0)
            step(PAIRS - 1, 1)
            step(PAIRS, 0)

        def fixed(t):
            return isinstance(t, int)

        def has_z(t):
            return not fixed(t) or 0 <= t < PAIRS

        def has(t, kind):
            pair = t + 1 if kind == "K" else t - 1 if fixed(t) else 0
            return not fixed(t) or 0 <= pair < PAIRS

        def count(t, kind, g):
            return t * G + (G + g + 1) if kind == "K" else t * G + (g + 1 - G)

        with nc.Block() as block:

            @block.sync
            def _(sp):
                def load(t, b, n):
                    c = bass.ds(t * P, P)
                    dst, sem = ((raw_k[:, b], f"raw_k{b}"), (raw_v, "raw_v"))[n]
                    past, new = caches[n]
                    sp.dma_start(dst[:, 0:TK - 1, :], past[:, :, c]).then_inc(s(sem), 16)
                    sp.dma_start(dst[0:DEC, TK - 1, :], new[:, c]).then_inc(s(sem), 16)
                    if not n:
                        sp.dma_start(raw_q[:, b, :], q_dram[SEQ:SEQ + DEC, c]).then_inc(s(sem), 16)

                def load_v(t, b):
                    sp.wait_ge(s("v_split"), t * 2 + 2)
                    load(t, b, 1)

                load(0, 0, 0)
                load(1, 1, 0)
                load_v(0, 0)
                with sp.Fori(0, 3) as i:
                    for n in (1, 2):
                        t = i * 2 + n
                        sp.wait_ge(s("K_turned"), t * G)
                        load(t + 1, (n + 1) % 2, 0)
                        load_v(t, n % 2)
                load_v(PAIRS - 1, 1)

            @block.tensor
            def _(pe):
                def bank_free(t, i):
                    before = [(t - 1, j) for j in range(len(ITEMS))] + [(t, j) for j in range(i)]
                    for at, j in reversed(before):
                        if j % BANKS == i % BANKS and has(at, ITEMS[j][0]) and (fixed(t) or i >= BANKS or ITEMS[j][0] == "K"):
                            kind, g = ITEMS[j]
                            pe.wait_ge(s(f"{kind}_lo"), count(at, kind, g) + (G if kind == "A" else 0))
                            break
                    if i == 1 and not fixed(t):
                        pe.wait_ge(s("A_lo"), count(t - 1, "A", G - 1) + G)

                def item(t, b, i):
                    kind, g = ITEMS[i]
                    if not has(t, kind):
                        return
                    bank_free(t, i)
                    hold(pe, s("pe_passed"))
                    if kind == "K":
                        for k in range(*GR[g]):
                            r = P if k < TK - 1 else DEC
                            last = nc.tensor.transpose(psR[:, i % BANKS, k % 4, 0:r], raw_k[0:r, 1 - b, k, :], ident[0:r, 0:r])
                        if g == G - 1:
                            last = nc.tensor.transpose(psR[:, i % BANKS, 1, 0:DEC], raw_q[:, 1 - b, :], ident[0:DEC, 0:DEC])
                    else:
                        for k in range(*GR[g]):
                            r = P if k < TK - 1 else DEC
                            last = nc.tensor.transpose(psR[0:r, i % BANKS, k % 4, :], wt[:, 1 - b, k * P:k * P + r],
                                                       ident[:, :])
                    last.then_inc(s(f"{kind}_turned"), 1)

                def z(t, b, g):
                    if not has_z(t):
                        return
                    c0, _, parts = ZG[g]
                    if g == 0:
                        pe.wait_ge(s("K_lo"), t * G + G)
                    pe.wait_ge(s("beta"), t * 3 + (g + 1))
                    at = 0
                    for n in parts:
                        c, out = slice(c0 + at, c0 + at + n), psZ[:, (3 * b + g) % 2, at:at + n]
                        last = three_passes(nc, out, q_hi[:], q_lo[:], kT_hi[:, c], kT_lo[:, c], True, True)
                        at += n
                    last.then_inc(s("z"), 1)

                def av(t, b):
                    if not has(t, "A"):
                        return
                    pe.wait_ge(s("A_lo"), t * G + G)
                    pe.wait_ge(s("v_split"), t * 2 + 2)
                    pe.wait_ge(s("y_sum"), t * 2)
                    for k in range(TK):
                        r = P if k < TK - 1 else DEC
                        for part in (1, 0):
                            last = nc.tensor.matmul(psY[:, 0:256], v2[0:r, 1 - b, k, part, :],
                                                    aT[0:r, k].rearrange("p a q -> p (a q)"),
                                                    start=(k == 0 and part == 1), stop=(k == TK - 1 and part == 0))
                    last.then_inc(s("av"), 1)

                def step(t, b):
                    if has(t, "K"):
                        pe.wait_ge(s(f"raw_k{1 - b}"), (t * 24 + 72) if b == 1 else (t * 24 + 48))
                    if has(t, "A"):
                        pe.wait_ge(s("weights"), t + 1)
                        pe.wait_ge(s("weights_low"), t + 1)
                    item(t, b, 0)
                    z(t, b, 0)
                    item(t, b, 1)
                    z(t, b, 1)
                    z(t, b, 2)
                    for i in range(2, len(ITEMS)):
                        item(t, b, i)
                    av(t, b)

                pe.sem_inc(s("av"), 2)
                bodies(pe, step)

            @block.scalar
            def _(act):
                def item(t, b, i):
                    kind, g = ITEMS[i]
                    if not has(t, kind):
                        return
                    k0, k1 = GR[g]
                    act.wait_ge(s(f"{kind}_turned"), count(t, kind, g))
                    if kind == "K":
                        c0, c1 = k0 * P, min(k1 * P, KEYS)
                        last = nc.scalar.activation(kT_hi[:, c0:c1], psR[:, i % BANKS].rearrange("p t c -> p (t c)")[:, 0:c1 - c0], ACT.Copy)
                        if g == G - 1:
                            for h in (slice(0, 64), slice(64, 128)):
                                last = nc.scalar.activation(q_hi[h, h], psR[h, i % BANKS, 1, 0:DEC], ACT.Copy)
                    else:
                        r = P if k0 < TK - 1 else DEC
                        if g == 0:
                            act.wait_ge(s("av"), t + 1)
                        last = nc.scalar.activation(aT[0:r, k0:k1, 0, :], psR[0:r, i % BANKS, 0:k1 - k0, :], ACT.Copy)
                    last.then_inc(s(f"{kind}_hi"), 1)

                def sigmoids(t, b, g):
                    if not has_z(t):
                        return
                    if g == 0:
                        act.wait_ge(s("scanned"), t + 1)
                    c0, n, _ = ZG[g]
                    act.wait_ge(s("z"), t * 3 + (g + 1))
                    src = psZ[:, (3 * b + g) % 2, 0:n]
                    nc.scalar.activation(nb[:, c0:c0 + n], src, ACT.Sigmoid, scale=-SCALE).then_inc(s("nb"), 1)
                    nc.scalar.activation(wt[:, b, c0:c0 + n], src, ACT.Sigmoid, scale=SCALE).then_inc(s("beta"), 1)

                def step(t, b):
                    item(t, b, 0)
                    sigmoids(t, b, 0)
                    item(t, b, 1)
                    sigmoids(t, b, 1)
                    sigmoids(t, b, 2)
                    for i in range(2, len(ITEMS)):
                        item(t, b, i)
                    if has(t, "A"):
                        act.wait_ge(s("av"), t + 2)
                        nc.scalar.activation(ytmp[:], psY[:, P:2 * P], ACT.Copy).then_inc(s("y_low"), 1)
                        act.wait_ge(s("y_sum"), t * 2 + 2)
                        nc.scalar.activation(ybT[0][:, bass.ds(t - 1, 1), SCOL:COLS].rearrange("p o c -> p (o c)"), yb[:],
                                             ACT.Copy).then_inc(s("yb_hi"), 1)

                act.wait_ge(s("cleared"), 1)
                act.sem_inc(s("beta"), 2)
                bodies(act, step)

            @block.gpsimd
            def _(pool):
                def link(ins):
                    link.n += 1
                    ins.then_inc(s("seen"), 1)
                    pool.wait_ge(s("seen"), link.n)

                link.n = 0
                first_half, second_half = seen[:, 0, :], seen[:, 1, :]
                link(nc.gpsimd.memset(seen[:], 1.0))
                link(nc.gpsimd.affine_select(out=first_half, in_=first_half, compare_op=ALU.is_gt, fill=0.0, base=0,
                                             pattern=[[-1, DEC]], channel_multiplier=1))
                link(nc.gpsimd.affine_select(out=first_half, in_=first_half, compare_op=ALU.is_ge, fill=0.0, base=DEC - 1,
                                             pattern=[[0, DEC]], channel_multiplier=-1))
                link(nc.gpsimd.affine_select(out=second_half, in_=second_half, compare_op=ALU.is_gt, fill=0.0, base=-DEC,
                                             pattern=[[-1, DEC]], channel_multiplier=1))
                link(nc.gpsimd.tensor_tensor(first_half, first_half, second_half, ALU.add))
                link(nc.gpsimd.tensor_scalar(second_half, first_half, -1.0, 1.0, ALU.mult, ALU.add))
                pool.sem_inc(s("v_split"), 2)
                pool.sem_inc(s("weights_low"), 1)
                with pool.Fori(0, PAIRS // 2) as i:
                    for b in range(2):
                        t = i * 2 + b
                        pool.wait_ge(s("raw_v"), t * 32 + 32)
                        pool.wait_ge(s("av"), t + 1)
                        hold(pool, s("pool_passed"))
                        for part in range(2):
                            if part:
                                pool.wait_ge(s("v_split"), t * 2 + 3)
                            for k, r in ((slice(0, TK - 1), P), (slice(TK - 1, TK), DEC)):
                                if part:
                                    last = nc.gpsimd.tensor_tensor(v2[0:r, b, k, 1, :], raw_v[0:r, k, :],
                                                                   v2[0:r, b, k, 0, :].bitcast(F32), ALU.subtract)
                                else:
                                    last = nc.gpsimd.tensor_scalar(v2[0:r, b, k, 0, :], raw_v[0:r, k, :], 1.0, 0.0,
                                                                   ALU.mult, ALU.add)
                            last.then_inc(s("v_split"), 1)
                        pool.wait_ge(s("scanned"), t + 2)
                        pool.wait_ge(s("beta"), t * 3 + 3)
                        nc.gpsimd.tensor_tensor(wt[:, b, 0:HALF], wt[:, b, 0:HALF], rest[:, 1:HALF + 1],
                                                ALU.mult).then_inc(s("weights_low"), 1)

            @block.vector
            def _(dve):
                def item(t, b, i):
                    kind, g = ITEMS[i]
                    if not has(t, kind):
                        return
                    k0, k1 = GR[g]
                    dve.wait_ge(s(f"{kind}_hi"), count(t, kind, g))
                    if kind == "K":
                        c0, c1 = k0 * P, min(k1 * P, KEYS)
                        last = nc.vector.tensor_tensor(kT_lo[:, c0:c1], psR[:, i % BANKS].rearrange("p t c -> p (t c)")[:, 0:c1 - c0],
                                                       kT_hi[:, c0:c1].bitcast(F32), ALU.subtract)
                        if g == G - 1:
                            for h in (slice(0, 64), slice(64, 128)):
                                last = nc.vector.tensor_tensor(q_lo[h, h], psR[h, i % BANKS, 1, 0:DEC], q_hi[h, h].bitcast(F32), ALU.subtract)
                    else:
                        r = P if k0 < TK - 1 else DEC
                        last = nc.vector.tensor_tensor(aT[0:r, k0:k1, 1, :], psR[0:r, i % BANKS, 0:k1 - k0, :],
                                                       aT[0:r, k0:k1, 0, :].bitcast(F32), ALU.subtract)
                    last.then_inc(s(f"{kind}_lo"), 1)

                def scan(t, b):
                    new = slice(PAST, KEYS)
                    dve.wait_ge(s("beta"), t * 3 + 5)
                    nc.vector.tensor_tensor(nb[:, new], nb[:, new], seen[:, 1, :], ALU.max).then_inc(s("masked"), 1)
                    nc.vector.tensor_tensor(wt[:, b, new], wt[:, b, new], seen[:, 0, :], ALU.mult).then_inc(s("masked"), 1)
                    dve.wait_ge(s("masked"), t * 2 + 1)
                    dve.wait_ge(s("weights"), t + 1)
                    dve.wait_ge(s("weights_low"), t + 1)
                    nc.vector.tensor_tensor_scan(rest[:, ::-1], nb[:, ::-1], nb[:, ::-1], 1.0, ALU.mult,
                                                 ALU.bypass).then_inc(s("scanned"), 1)

                def weigh(t, b):
                    dve.wait_ge(s("masked"), t * 2 + 2)
                    dve.wait_ge(s("scanned"), t + 2)
                    nc.vector.tensor_tensor(wt[:, b, HALF:KEYS - 1], wt[:, b, HALF:KEYS - 1], rest[:, HALF + 1:KEYS],
                                            ALU.mult).then_inc(s("weights"), 1)

                def step(t, b):
                    item(t, b, 0)
                    item(t, b, 1)
                    if has_z(t):
                        scan(t, b)
                    for i in range(2, len(ITEMS)):
                        item(t, b, i)
                        if i == 4 and has_z(t):
                            weigh(t, b)
                    if has(t, "A"):
                        dve.wait_ge(s("y_low"), t)
                        for h in (slice(0, 64), slice(64, 128)):
                            nc.vector.tensor_tensor(yb[h, :], psY[h, h], ytmp[h, h], ALU.add).then_inc(s("y_sum"), 1)
                        dve.wait_ge(s("yb_hi"), t)
                        nc.vector.tensor_tensor(ybT[1][:, bass.ds(t - 1, 1), SCOL:COLS].rearrange("p o c -> p (o c)"), yb[:],
                                                ybT[0][:, bass.ds(t - 1, 1), SCOL:COLS].rearrange("p o c -> p (o c)").bitcast(F32),
                                                ALU.subtract).then_inc(s("yb_lo"), 1)

                dve.wait_ge(s("seen"), 6)
                dve.sem_inc(s("scanned"), 1)
                dve.sem_inc(s("weights"), 1)
                dve.sem_inc(s("A_lo"), G)
                dve.sem_inc(s("y_sum"), 2)
                nc.vector.memset(q_hi[:].bitcast(F32), 0.0)
                nc.vector.memset(q_lo[:].bitcast(F32), 0.0).then_inc(s("cleared"), 1)
                bodies(dve, step)


def phase_merge(nc, a, ybT, mgT, ta_dram, gb_dram, rf, rf_size):
    w_b = a["w_branch_b"][0].rearrange("(k p) c -> p k c", p=P)
    with ExitStack() as ctx:
        s = Sems(nc, ctx, "p6")
        f = Place(nc, rf, rf_size)
        ring = Weights(nc, s, Weights.buffers("p6", 4, f, f))
        ta = f("p6_ta", [P, 2, COLS])
        gb = f("p6_gb", [P, 2, COLS])
        ps = ctx.enter_context(nc.psum_tensor("p6_ps", [P, 2, 4, 512], F32))
        U = 4
        with nc.Block() as block:

            @block.sync
            def _(sp):
                with sp.Fori(0, KT // U) as i:
                    for n in range(U):
                        ring.load(sp, i * U + n, n % 2, w_b[:, :, bass.ds(i * U * P + n * P, P)], KT)

            @block.gpsimd
            def _(pool):
                ring.start_pool(pool)
                with pool.Fori(0, KT // U) as i:
                    for n in range(U):
                        pool.wait_ge(s("product"), i * U + (n + 1))
                        ring.split_one(pool, i * U + n, i * 2 + n // 2, n, n % 2)

            @block.tensor
            def _(pe):
                pe.sem_inc(s("product"), U)
                with pe.Fori(0, KT // U) as i:
                    for n in range(U):
                        ring.ready(pe, i * U + n)
                        pe.wait_ge(s("gated"), i * U + (n + 1))
                        feature_product(nc, pe, ps[:, n % 2], ring, n, ybT).then_inc(s("product"), 1)

            @block.scalar
            def _(act):
                act.sem_inc(s("merged_hi"), 2)
                with act.Fori(0, KT // U) as i:
                    for n in range(U):
                        j = i * U + n
                        act.wait_ge(s("merged_lo"), i * U + (n + 1))
                        act.dma_start(ta[:, n % 2, :], ta_dram[bass.ds(j, 1), :, :].rearrange("o p c -> (o p) c")).then_inc(s(f"ta_ready{n % 2}"), 16)
                        act.dma_start(gb[:, n % 2, :], gb_dram[bass.ds(j, 1), :, :].rearrange("o p c -> (o p) c")).then_inc(s(f"gb_ready{n % 2}"), 16)
                        act.wait_ge(s("merged"), i * U + (n + 1))
                        nc.scalar.activation(mgT[0][:, bass.ds(j, 1), GAP:COLS].rearrange("p o c -> p (o c)"), ta[:, n % 2, GAP:COLS],
                                             ACT.Copy).then_inc(s("merged_hi"), 1)

            @block.vector
            def _(dve):
                dve.sem_inc(s("gated"), 2)
                dve.sem_inc(s("merged_lo"), 2)
                with dve.Fori(0, KT // U) as i:
                    for n in range(U):
                        j = i * U + n
                        dve.wait_ge(s("product"), i * U + (n + U + 1))
                        dve.wait_ge(s(f"gb_ready{n % 2}"), (i * (U // 2) + (n // 2 + 1)) * 16)
                        g = by_chunks(gb[:, n % 2, :])
                        nc.vector.tensor_tensor(g, ps[:, n % 2, 0:NCH, 0:CH], g, ALU.mult).then_inc(s("gated"), 1)
                        dve.wait_ge(s("gated"), i * U + (n + 3))
                        dve.wait_ge(s(f"ta_ready{n % 2}"), (i * (U // 2) + (n // 2 + 1)) * 16)
                        nc.vector.tensor_tensor(ta[:, n % 2, :], ta[:, n % 2, :], gb[:, n % 2, :], ALU.add).then_inc(s("merged"), 1)
                        dve.wait_ge(s("merged"), i * U + (n + 1))
                        dve.wait_ge(s("merged_hi"), i * U + (n + 3))
                        nc.vector.tensor_tensor(mgT[1][:, bass.ds(j, 1), GAP:COLS].rearrange("p o c -> p (o c)"), ta[:, n % 2, GAP:COLS],
                                                mgT[0][:, bass.ds(j, 1), GAP:COLS].rearrange("p o c -> p (o c)").bitcast(F32),
                                                ALU.subtract).then_inc(s("merged_lo"), 1)


def phase_output(nc, a, ident, mgT, x2_dram, ffn_ring, r0, r0_size, rf, rf_size):
    w_o = a["w_o"][0].rearrange("(k p) c -> p k c", p=P)
    w_up = a["w_up"][0].rearrange("(k p) c -> p k c", p=P)
    h2T = mgT
    RAW = 4
    LAG = 2
    with ExitStack() as ctx:
        s = Sems(nc, ctx, "p7")
        AHEAD, SLOT_BYTES = Weights.AHEAD, SLOT * 4
        next_raw, next_hi, next_lo = ffn_ring
        hi_at = rf + 2 * SLOT_BYTES
        lo_at = hi_at + FFN_SLOTS * SLOT_BYTES
        g = Place(nc, hi_at + AHEAD * SLOT_BYTES, (FFN_SLOTS - AHEAD) * SLOT_BYTES)
        f = Place(nc, lo_at + AHEAD * SLOT_BYTES, rf + rf_size - lo_at - AHEAD * SLOT_BYTES)
        w = Place(nc, r0, r0_size)
        w_hi = w("p7_w_hi", [P, 8, SLOT], F32R)
        w_lo = w("p7_w_lo", [P, 8, SLOT], F32R)
        g_post = f("g_post_row", [P, D])
        g_ffn = f("g_ffn_row", [P, D])
        x = g("p7_x", [P, 2, D])
        y = f("p7_y", [P, 2, D])
        h2 = f("p7_h2", [P, 2, D])
        junk = f("p7_squares", [P, D])
        own_raw = g("p7_w_raw", [P, RAW - 2, SLOT])
        w_raw = [next_raw[:, 0, :], next_raw[:, 1, :], own_raw[:, 0, :], own_raw[:, 1, :]]
        ss = f("p7_ss", [P, 2, 2])
        rstd = f("p7_rstd", [P, 2, 2])
        tmp = f("p7_tmp", [P, 2, 2])
        ps = ctx.enter_context(nc.psum_tensor("p7_ps", [P, 2, D], F32))
        psT = ctx.enter_context(nc.psum_tensor("p7_psT", [P, 2, KT, P], F32))
        with nc.Block() as block:

            @block.sync
            def _(sp):
                for n in range(8):
                    if n >= RAW:
                        sp.wait_ge(s("w_lo"), n - RAW + 1)
                    sp.dma_start(w_raw[n % RAW].rearrange("p (k c) -> p k c", k=2),
                                 w_o[:, 2 * (n % 4):2 * (n % 4) + 2, (n // 4) * 512:(n // 4 + 1) * 512]).then_inc(s(f"raw_ready{n % RAW}"), 16)
                for n in range(AHEAD):
                    if n == 0:
                        sp.wait_ge(s("w_lo"), RAW + AHEAD)
                    sp.dma_start(next_raw[:, n, :].rearrange("p (k c) -> p k c", k=KT),
                                 w_up[:, :, n * FF:n * FF + P]).then_inc(s(f"next_ready{n}"), 16)
                sp.dma_start(g_post[:], a["g_post_mix"].to_broadcast([P, D])).then_inc(s("g_ready"), 16)
                sp.dma_start(g_ffn[:], a["g_pre_ffn"].to_broadcast([P, D])).then_inc(s("g_ready"), 16)
                for m in range(TILES):
                    if m >= 2:
                        sp.wait_ge(s("x2_ready"), m - 1)
                    src = a["x_prompt"][0, m * P:(m + 1) * P, :] if m < TILES - 1 else a["x_sample"][0]
                    sp.dma_start(x[0:rows(m), m % 2, :], src).then_inc(s(f"x_ready{m % 2}"), 16)

            @block.gpsimd
            def _(pool):
                for n in range(AHEAD):
                    pool.wait_ge(s(f"next_ready{n}"), 16)
                    nc.gpsimd.tensor_scalar(next_hi[:, n, :], next_raw[:, n, :], 1.0, 0.0, ALU.mult, ALU.add).then_inc(s("next_split"), 1)
                    pool.wait_ge(s("next_split"), 2 * n + 1)
                    nc.gpsimd.tensor_tensor(next_lo[:, n, :], next_raw[:, n, :], next_hi[:, n, :].bitcast(F32),
                                            ALU.subtract).then_inc(s("next_split"), 1)
                for m in range(TILES):
                    pool.wait_ge(s("x2_ready"), m + 1)
                    pool.dma_start(x2_dram[m * P:m * P + rows(m), :], y[0:rows(m), m % 2, :]).then_inc(s(f"x2_stored{m % 2}"), 16)
                pool.wait_ge(s("x2_stored0"), 16 * 5)
                pool.wait_ge(s("x2_stored1"), 16 * 4)

            @block.tensor
            def _(pe):
                def product(m):
                    for c in range(2):
                        if m >= 2 and c == 0:
                            pe.wait_ge(s("y_scaled"), m - 1)
                        for k in range(KT):
                            slot, at = 4 * c + k // 2, (k % 2) * 512
                            if m == 0 and k % 2 == 0:
                                pe.wait_ge(s("w_lo"), slot + 1)
                            last = three_passes(
                                nc, ps[0:rows(m), m % 2, c * 512:(c + 1) * 512], mgT[0][:, k, col(m):col(m) + rows(m)],
                                mgT[1][:, k, col(m):col(m) + rows(m)], w_hi[:, slot, at:at + 512],
                                w_lo[:, slot, at:at + 512], k == 0, k == KT - 1)
                    last.then_inc(s("product"), 1)

                def turn(m):
                    pe.wait_ge(s("h2_ready"), m + 1)
                    if m >= 2:
                        pe.wait_ge(s("h2T_lo"), m - 1)
                    for k in range(KT):
                        last = nc.tensor.transpose(psT[:, m % 2, k, 0:rows(m)], h2[0:rows(m), m % 2, k * P:(k + 1) * P],
                                                   ident[0:rows(m), 0:rows(m)])
                    last.then_inc(s("h2_turned"), 1)

                product(0)
                product(1)
                for m in range(TILES):
                    if m + 2 < TILES:
                        product(m + 2)
                    turn(m)

            @block.scalar
            def _(act):
                def hi(m):
                    act.wait_ge(s("h2_turned"), m + 1)
                    nc.scalar.activation(h2T[0][:, :, col(m):col(m) + rows(m)], psT[:, m % 2, :, 0:rows(m)],
                                         ACT.Copy).then_inc(s("h2T_hi"), 1)

                for n in range(8):
                    act.wait_ge(s(f"raw_ready{n % RAW}"), 16 * (n // RAW + 1))
                    nc.scalar.activation(w_hi[:, n, :], w_raw[n % RAW], ACT.Copy).then_inc(s("w_hi"), 1)
                act.wait_ge(s("ss_set"), 1)
                for m in range(TILES):
                    r = rows(m)
                    act.wait_ge(s("product"), m + 1)
                    if m >= 2:
                        act.wait_ge(s("h2_ready"), m - 1)
                    nc.scalar.activation(junk[0:r, :], ps[0:r, m % 2, :], ACT.Square,
                                         accum_out=ss[0:r, m % 2, 0:1]).then_inc(s("squares"), 1)
                    act.wait_ge(s("squares"), 2 * m + 1)
                    if m >= LAG:
                        hi(m - LAG)
                    act.wait_ge(s("x2_ready"), m + 1)
                    nc.scalar.activation(junk[0:r, :], y[0:r, m % 2, :], ACT.Square,
                                         accum_out=ss[0:r, m % 2, 1:2]).then_inc(s("squares"), 1)
                    act.wait_ge(s("squares"), 2 * m + 2)
                for m in range(TILES - LAG, TILES):
                    hi(m)

            @block.vector
            def _(dve):
                for n in range(8):
                    dve.wait_ge(s("w_hi"), n + 1)
                    nc.vector.tensor_tensor(w_lo[:, n, :], w_raw[n % RAW], w_hi[:, n, :].bitcast(F32),
                                            ALU.subtract).then_inc(s("w_lo"), 1)
                ch = Chain(dve, s("dve_chain"))
                nc.vector.memset(ss[:], 1.0).then_inc(s("ss_set"), 1)
                ch.step(clear_gaps(nc, nc.vector, *h2T))
                dve.wait_ge(s("g_ready"), 32)

                def lo(m):
                    c = slice(col(m), col(m) + rows(m))
                    dve.wait_ge(s("h2T_hi"), m + 1)
                    nc.vector.tensor_tensor(h2T[1][:, :, c], psT[:, m % 2, :, 0:rows(m)], h2T[0][:, :, c].bitcast(F32),
                                            ALU.subtract).then_inc(s("h2T_lo"), 1)

                for m in range(TILES):
                    r, b = rows(m), m % 2
                    dve.wait_ge(s("squares"), 2 * m + 1)
                    rsqrt_steps(nc, ch, ss[0:r, b, 0:1], rstd[0:r, b, 0:1], tmp[0:r, b, 0:1], 1.0 / D)
                    if m >= 2:
                        dve.wait_ge(s(f"x2_stored{b}"), 16 * (m // 2))
                    nc.vector.scalar_tensor_tensor(out=y[0:r, b, :], in0=ps[0:r, b, :], scalar=rstd[0:r, b, 0:1],
                                                   in1=g_post[0:r, :], op0=ALU.mult, op1=ALU.mult).then_inc(s("y_scaled"), 1)
                    dve.wait_ge(s("y_scaled"), m + 1)
                    dve.wait_ge(s(f"x_ready{b}"), 16 * (m // 2 + 1))
                    nc.vector.tensor_tensor(y[0:r, b, :], y[0:r, b, :], x[0:r, b, :], ALU.add).then_inc(s("x2_ready"), 1)
                    if m >= LAG:
                        lo(m - LAG)
                    dve.wait_ge(s("squares"), 2 * m + 2)
                    rsqrt_steps(nc, ch, ss[0:r, b, 1:2], rstd[0:r, b, 1:2], tmp[0:r, b, 1:2], 1.0 / D)
                    if m >= 2:
                        dve.wait_ge(s("h2_turned"), m - 1)
                    nc.vector.scalar_tensor_tensor(out=h2[0:r, b, :], in0=y[0:r, b, :], scalar=rstd[0:r, b, 1:2],
                                                   in1=g_ffn[0:r, :], op0=ALU.mult, op1=ALU.mult).then_inc(s("h2_ready"), 1)
                for m in range(TILES - LAG, TILES):
                    lo(m)


def phase_ffn(nc, a, o, ident, par, h2T, x2_dram, ffn_ring, ffn_ring_end, r0, r0_size, rf, rf_size):
    w_up = a["w_up"][0].rearrange("(k p) c -> p k c", p=P)
    w_down = a["w_down"][0].rearrange("(f p) c -> f p c", p=P)
    SHARES = 2 * TILES
    CHUNKS = 2 * NCH
    BANKS = 4
    LAST = SCOL + DEC
    AHEAD = Weights.AHEAD
    EARLY = 6
    with ExitStack() as ctx:
        s = Sems(nc, ctx, "p8")
        f_ = Place(nc, ffn_ring_end, rf + rf_size - ffn_ring_end)
        r_ = Place(nc, r0, r0_size)
        ring = Weights(nc, s, ffn_ring)
        acc = r_("p8_acc", [P, TILES, D])
        hid_hi = r_("p8_hid_hi", [P, COLS], F32R)
        hid_lo = r_("p8_hid_lo", [P, COLS], F32R)
        x = [r_("p8_up_gate", [P, COLS]), r_("p8_up_val", [P, COLS])]
        cv = [r_("p8_conv_gate", [P, COLS]), f_("p8_conv_val", [P, COLS])]
        tails = f_("p8_tails", [P, 4, 2 * FT])
        tail_rows = f_("p8_tail_rows", [2 * FT, 4, P])
        ss = r_("p8_ss", [P, TILES])
        rstd = r_("p8_rstd", [P, TILES])
        tmp = r_("p8_tmp", [P, TILES])
        r1 = r0 + r0_size
        x2 = nc.alloc_sbuf_tensor_at("p8_x2", [P, TILES, D], F32, offset=r1)
        g_row = nc.alloc_sbuf_tensor_at("p8_g_row", [P, D], F32, offset=r1 + TILES * D * 4)
        junk = nc.alloc_sbuf_tensor_at("p8_squares", [P, D], F32, offset=r1 + (TILES + 1) * D * 4)
        psU = ctx.enter_context(nc.psum_tensor("p8_psU", [P, BANKS, 512], F32))
        psD = ctx.enter_context(nc.psum_tensor("p8_psD", [P, BANKS, 512], F32))
        state = par[:, PAR["state0"]:PAR["state0"] + 4 * FT].rearrange("p (j t) -> p j t", j=2)

        def up_bank(b, kind, c):
            return (b * CHUNKS + kind * NCH + c) % BANKS

        def share_bank(b, n):
            return (b * SHARES + n) % BANKS

        def bodies(eng, step, tail):
            step(0, 0, True)
            step(1, 1, False)
            with eng.Fori(1, FT // 2) as i:
                step(i * 2, 0, False)
                step(i * 2 + 1, 1, False)
            tail(FT - 1, 1)

        with nc.Block() as block:

            @block.sync
            def _(sp):
                def step(f, b, first):
                    for kind in range(AHEAD if first else 0, 3):
                        src = (w_up[:, :, bass.ds(f * P + kind * FF, P)] if kind < 2
                               else w_down[bass.ds(f, 1), :, :].rearrange("o p (k c) -> (o p) k c", k=KT))
                        ring.load(sp, f * 3 + kind, (3 * b + kind) % 2, src, KT)

                ring.start_ahead(sp)
                bodies(sp, step, lambda f, b: None)
                sp.wait_ge(s("up"), CHUNKS * (FT + 2))
                sp.dma_start(g_row[:], a["g_post_ffn"].to_broadcast([P, D])).then_inc(s("g_ready"), 16)
                for m in range(TILES):
                    sp.dma_start(x2[0:rows(m), m, :], x2_dram[m * P:m * P + rows(m), :]).then_inc(s("x2_ready"), 16)
                for m in (0, 1, 6, 2, 7, 3, 8, 4, 5):
                    if m < EARLY:
                        sp.wait_ge(s("dve_added"), m + 1)
                    else:
                        sp.wait_ge(s("pool_added"), m - EARLY + 1)
                    dst = o["y_prompt"][0, m * P:(m + 1) * P, :] if m < TILES - 1 else o["y_sample"][0]
                    sp.dma_start(dst, x2[0:rows(m), m, :]).then_inc(s("stored"), 16)
                sp.wait_ge(s("stored"), 16 * TILES)

            @block.gpsimd
            def _(pool):
                def step(f, b, first):
                    for kind in range(AHEAD if first else 0, 3):
                        if kind < 2:
                            pool.wait_ge(s("up"), f * CHUNKS + (kind + 1) * NCH)
                        else:
                            pool.wait_ge(s("share"), f * SHARES + SHARES)
                        n = 3 * b + kind
                        ring.split_one(pool, f * 3 + kind, (f - b) * 3 // 2 + n // 2, n, n % 2)

                ring.start_pool(pool, AHEAD)
                bodies(pool, step, lambda f, b: None)
                pool.wait_ge(s("g_ready"), 16)
                for m in range(EARLY):
                    pool.wait_ge(s("squares"), m + 1)
                    nc.gpsimd.tensor_tensor(acc[0:rows(m), m, :], acc[0:rows(m), m, :], g_row[0:rows(m), :],
                                            ALU.mult).then_inc(s("times_g"), 1)
                for n, m in enumerate(range(EARLY, TILES)):
                    pool.wait_ge(s("scaled"), n + 1)
                    nc.gpsimd.tensor_tensor(x2[0:rows(m), m, :], x2[0:rows(m), m, :], acc[0:rows(m), m, :],
                                            ALU.add).then_inc(s("pool_added"), 1)

            @block.tensor
            def _(pe):
                def up(f, b, kind):
                    ring.ready(pe, f * 3 + kind)
                    slot = 3 * b + kind
                    for c in range(NCH):
                        pe.wait_ge(s("up_taken"), f * CHUNKS + (kind * NCH + c + 1))
                        cols = slice(c * CH, (c + 1) * CH)
                        for k in range(KT):
                            w = slice(k * P, (k + 1) * P)
                            last = three_passes(nc, psU[:, up_bank(b, kind, c), 0:CH], ring.hi[:, slot, w], ring.lo[:, slot, w],
                                                h2T[0][:, k, cols], h2T[1][:, k, cols], k == 0, k == KT - 1)
                        last.then_inc(s("up"), 1)

                def down(f, b):
                    ring.ready(pe, f * 3 + 2)
                    pe.wait_ge(s("hid_lo"), f + 2)
                    slot = 3 * b + 2
                    for m in range(TILES):
                        r, c = rows(m), slice(col(m), col(m) + rows(m))
                        for h in range(2):
                            n = 2 * m + h
                            pe.wait_ge(s("added"), f * SHARES + (n + 1))
                            w = slice(h * 512, (h + 1) * 512)
                            three_passes(nc, psD[0:r, share_bank(b, n), :], hid_hi[:, c], hid_lo[:, c], ring.hi[:, slot, w],
                                         ring.lo[:, slot, w], True, True).then_inc(s("share"), 1)

                def step(f, b, first):
                    up(f, b, 0)
                    if not first:
                        down(f - 1, 1 - b)
                    up(f, b, 1)

                pe.sem_inc(s("up"), 2 * CHUNKS)
                pe.sem_inc(s("share"), 2 * SHARES)
                bodies(pe, step, down)
                pe.wait_ge(s("up_taken"), CHUNKS * FT + BANKS)
                pe.wait_ge(s("tails"), 2 * FT)
                for j in range(4):
                    last = nc.tensor.transpose(psU[0:2 * FT, 0, j * P:(j + 1) * P], tails[:, j, :], ident[:, :])
                last.then_inc(s("tails_turned"), 1)

            @block.scalar
            def _(act):
                def step(f, b, first):
                    for kind in range(2):
                        for c in range(NCH):
                            n = kind * NCH + c
                            act.wait_ge(s("up"), f * CHUNKS + (n + 1 + 2 * CHUNKS))
                            if c == 0:
                                act.wait_ge(s("conv"), f * 2 + (kind + 1))
                            nc.scalar.activation(x[kind][:, c * CH:(c + 1) * CH], psU[:, up_bank(b, kind, c), 0:CH],
                                                 ACT.Copy).then_inc(s("up_taken"), 1)
                        act.wait_ge(s("up_taken"), f * CHUNKS + (n + 1 + BANKS))
                        if kind == 0:
                            act.wait_ge(s("hid_lo"), f + 1)
                        else:
                            act.wait_ge(s("hid"), f + 1)
                        at = kind * FT
                        nc.scalar.activation(cv[kind][:, GAP:COLS], x[kind][:, GAP:COLS], ACT.Identity,
                                             scale=par[:, bass.ds(f + (PAR["w_conv2"] + at), 1)],
                                             bias=par[:, bass.ds(f + (PAR["b_conv"] + at), 1)]).then_inc(s("conv_begun"), 1)
                        if kind == 0:
                            act.wait_ge(s("conv"), f * 2 + 3)
                            nc.scalar.activation(cv[0][:, GAP:COLS], cv[0][:, GAP:COLS], ACT.Gelu_apprx_tanh).then_inc(s("gelu"), 1)
                    act.wait_ge(s("hid"), f + 2)
                    nc.scalar.activation(hid_hi[:, GAP:COLS], cv[0][:, GAP:COLS], ACT.Copy).then_inc(s("hid_hi"), 1)

                act.sem_inc(s("up_taken"), BANKS)
                bodies(act, step, lambda f, b: None)
                for m in range(TILES):
                    act.wait_ge(s("added"), (FT - 1) * SHARES + (2 * m + 2 + BANKS))
                    nc.scalar.activation(junk[0:rows(m), :], acc[0:rows(m), m, :], ACT.Square,
                                         accum_out=ss[0:rows(m), m:m + 1]).then_inc(s("squares"), 1)
                    act.wait_ge(s("squares"), m + 1)
                act.wait_ge(s("tails_turned"), 1)
                nc.scalar.activation(tail_rows[:], psU[0:2 * FT, 0, :].rearrange("p (j c) -> p j c", j=4), ACT.Copy).then_inc(s("tail_rows"), 1)
                act.wait_ge(s("tail_rows"), 1)
                for j in range(4):
                    dst = o["new_conv_prompt" if j < 2 else "new_conv_sample"][0, 0, j % 2].rearrange("(t c) -> t c", c=P)
                    act.dma_start(dst, tail_rows[:, j, :]).then_inc(s("tails_stored"), 16)
                act.wait_ge(s("tails_stored"), 16 * 4)

            @block.vector
            def _(dve):
                def add_share(f, b):
                    for m in range(TILES):
                        for h in range(2):
                            n, r = 2 * m + h, rows(m)
                            w = slice(h * 512, (h + 1) * 512)
                            dve.wait_ge(s("share"), f * SHARES + (n + 1 + 2 * SHARES))
                            nc.vector.tensor_tensor(acc[0:r, m, w], psD[0:r, share_bank(b, n), :], acc[0:r, m, w],
                                                    ALU.add).then_inc(s("added"), 1)

                def convolve(f, kind):
                    at, xk, ck = kind * FT, x[kind], cv[kind]
                    dve.wait_ge(s("conv_begun"), f * 2 + (kind + 1))
                    nc.vector.tensor_copy(tails[:, 0:2, bass.ds(f + at, 1)], xk[:, GAP + SEQ - 2:GAP + SEQ].unsqueeze(2))
                    nc.vector.tensor_copy(tails[:, 2:4, bass.ds(f + at, 1)], xk[:, LAST - 2:LAST].unsqueeze(2)).then_inc(s("tails"), 1)
                    nc.vector.tensor_copy(xk[:, GAP + SEQ:SCOL].unsqueeze(2), state[:, :, bass.ds(f + at, 1)]).then_inc(s("history"), 1)
                    dve.wait_ge(s("history"), f * 2 + (kind + 1))
                    for j in (1, 0):
                        ins = nc.vector.scalar_tensor_tensor(
                            out=ck[:, GAP:COLS], in0=xk[:, j:COLS - GAP + j],
                            scalar=par[:, bass.ds(f + (PAR[f"w_conv{j}"] + at), 1)], in1=ck[:, GAP:COLS],
                            op0=ALU.mult, op1=ALU.add)
                        if j:
                            ins.then_inc(s("conv_half"), 1)
                            dve.wait_ge(s("conv_half"), f * 2 + (kind + 1))
                    ins.then_inc(s("conv"), 1)

                def step(f, b, first):
                    if not first:
                        add_share(f - 1, 1 - b)
                    convolve(f, 0)
                    convolve(f, 1)
                    dve.wait_ge(s("gelu"), f + 1)
                    dve.wait_ge(s("conv"), f * 2 + 4)
                    nc.vector.tensor_tensor(cv[0][:, GAP:COLS], cv[0][:, GAP:COLS], cv[1][:, GAP:COLS], ALU.mult).then_inc(s("hid"), 1)
                    dve.wait_ge(s("hid_hi"), f + 1)
                    nc.vector.tensor_tensor(hid_lo[:, GAP:COLS], cv[0][:, GAP:COLS], hid_hi[:, GAP:COLS].bitcast(F32),
                                            ALU.subtract).then_inc(s("hid_lo"), 1)

                dve.sem_inc(s("conv"), 2)
                dve.sem_inc(s("hid"), 1)
                dve.sem_inc(s("hid_lo"), 1)
                dve.sem_inc(s("added"), BANKS)
                nc.vector.memset(acc[:], 0.0)
                nc.vector.memset(ss[:], 1.0).then_inc(s("acc_clear"), 1)
                dve.wait_ge(s("acc_clear"), 1)
                bodies(dve, step, add_share)
                dve.wait_ge(s("squares"), TILES)
                ch = Chain(dve, s("dve_chain"))
                rsqrt_steps(nc, ch, ss[:], rstd[:], tmp[:], 1.0 / D)
                dve.wait_ge(s("x2_ready"), 16 * TILES)
                dve.wait_ge(s("g_ready"), 16)
                for m in (0, 6, 1, 7, 2, 8, 3, 4, 5):
                    r = rows(m)
                    if m < EARLY:
                        dve.wait_ge(s("times_g"), m + 1)
                        nc.vector.scalar_tensor_tensor(out=x2[0:r, m, :], in0=acc[0:r, m, :], scalar=rstd[0:r, m:m + 1],
                                                       in1=x2[0:r, m, :], op0=ALU.mult, op1=ALU.add).then_inc(s("dve_added"), 1)
                    else:
                        nc.vector.scalar_tensor_tensor(out=acc[0:r, m, :], in0=acc[0:r, m, :], scalar=rstd[0:r, m:m + 1],
                                                       in1=g_row[0:r, :], op0=ALU.mult, op1=ALU.mult).then_inc(s("scaled"), 1)


_INS = ["x_prompt", "x_sample", "cache_sb_k", "cache_sb_v", "state_ffn_conv", "g_pre_mix", "w_in", "ln_v_g", "ln_v_b",
        "w_s", "b_s", "w_gate", "b_gate", "w_branch_a", "w_branch_b", "w_o", "g_post_mix", "g_pre_ffn", "w_up",
        "w_conv", "b_conv", "w_down", "g_post_ffn"]
_OUTS = [("y_prompt", (1, SEQ, D)), ("y_sample", (1, DEC, D)),
         ("new_sb_k_prompt", (1, 1, SEQ, HEADS, DH)), ("new_sb_v_prompt", (1, 1, SEQ, HEADS, DH)),
         ("new_conv_prompt", (1, 1, 2, 2 * FF)),
         ("new_sb_k_sample", (1, 1, DEC, HEADS, DH)), ("new_sb_v_sample", (1, 1, DEC, HEADS, DH)),
         ("new_conv_sample", (1, 1, 2, 2 * FF)), ("new_gmlp_v_sample", (1, 1, DEC, D))]


def kernel(**inputs):
    import numpy as _np
    import concourse.bacc as _bacc
    from concourse import mybir as _mybir
    from concourse.bass_utils import run_bass_kernel_spmd as _run

    nc = _bacc.Bacc("TRN2", target_bir_lowering=False, num_devices=1)
    arrays, ins, outs = {}, {}, {}
    for name in _INS:
        v = _np.ascontiguousarray(inputs[name])
        arrays[f"in_{name}"] = v
        ins[name] = nc.dram_tensor(f"in_{name}", v.shape, _mybir.dt.from_np(v.dtype), kind="ExternalInput").ap()
    for name, shape in _OUTS:
        outs[name] = nc.dram_tensor(f"out_{name}", shape, _mybir.dt.float32, kind="ExternalOutput").ap()
    build_layer(nc, ins, outs)
    r = _run(nc, [arrays], core_ids=[0])
    return tuple(r.results[0][f"out_{name}"] for name, _ in _OUTS)
```
